# Optimizing a Trainium2 kernel written in Bass

```python
import jax, jax.numpy as jnp
from jax import lax
import numpy as np

D_MODEL = 1024
BATCH = 1
SEQ = 256
DEPTH = 2
DEC_BATCH = 1
DEC_SEQ = 512
PAST_LEN = 128

N_MIXERS = 2
D_FF = 2816
FFN_RESIDUAL_WEIGHT = 0.5
CONV_WIDTH = 31
CONV_HALF = CONV_WIDTH // 2
N_HEADS = 8
QK_NOPE_DIM = 128
QK_ROPE_DIM = 64
V_HEAD_DIM = 128
Q_LORA_RANK = 384
KV_LORA_RANK = 256
ROPE_THETA = 10000.0
Q_BLOCK = 128
NORM_EPS = 1e-6

kernel_name = 'hybrid_conformer_mla_encoder'

def rms_norm(x, g):
    xf = x.astype(jnp.float32)
    y = xf * lax.rsqrt(jnp.mean(xf * xf, axis=-1, keepdims=True) + NORM_EPS)
    return (y * g.astype(jnp.float32)).astype(x.dtype)

def layer_norm(x, g, b):
    xf = x.astype(jnp.float32)
    mu = jnp.mean(xf, axis=-1, keepdims=True)
    var = jnp.mean(jnp.square(xf - mu), axis=-1, keepdims=True)
    y = (xf - mu) * lax.rsqrt(var + NORM_EPS)
    return (y * g.astype(jnp.float32) + b.astype(jnp.float32)).astype(x.dtype)

def swiglu(x, w_gate, w_up, w_down):
    return (jax.nn.silu(x @ w_gate) * (x @ w_up)) @ w_down

def conv_module(x, w_pw1, b_pw1, w_dw, b_dw, ln_g, ln_b, w_pw2, b_pw2):
    h = x @ w_pw1 + b_pw1
    h = h[..., :D_MODEL] * jax.nn.sigmoid(h[..., D_MODEL:])
    h = lax.conv_general_dilated(
        h, w_dw[:, None, :], window_strides=(1,), padding=[(CONV_HALF, CONV_HALF)],
        dimension_numbers=('NWC', 'WIO', 'NWC'), feature_group_count=D_MODEL) + b_dw
    h = jax.nn.silu(layer_norm(h, ln_g, ln_b))
    return h @ w_pw2 + b_pw2

def rope_tables(seq):
    pos = jnp.arange(seq, dtype=jnp.float32)
    inv_freq = ROPE_THETA ** (-jnp.arange(0, QK_ROPE_DIM, 2, dtype=jnp.float32) / QK_ROPE_DIM)
    ang = pos[:, None] * inv_freq[None, :]
    return jnp.cos(ang), jnp.sin(ang)

def apply_rope(x, cos, sin):
    half = QK_ROPE_DIM // 2
    x1, x2 = x[..., :half], x[..., half:]
    out = jnp.concatenate([x1 * cos - x2 * sin, x2 * cos + x1 * sin], axis=-1)
    return out.astype(x.dtype)

def mla(x, w_dq, q_norm_g, w_uq, w_dkv, kv_norm_g, w_uk, w_uv, w_o):
    B, S, _ = x.shape
    cos, sin = rope_tables(S)
    c_q = rms_norm(x @ w_dq, q_norm_g)
    q = (c_q @ w_uq).reshape(B, S, N_HEADS, QK_NOPE_DIM + QK_ROPE_DIM)
    q_nope = q[..., :QK_NOPE_DIM]
    q_rope = apply_rope(q[..., QK_NOPE_DIM:], cos[:, None, :], sin[:, None, :])
    kv_a = x @ w_dkv
    c_kv = rms_norm(kv_a[..., :KV_LORA_RANK], kv_norm_g)
    k_rope = apply_rope(kv_a[..., KV_LORA_RANK:], cos, sin)
    k_nope = (c_kv @ w_uk).reshape(B, S, N_HEADS, QK_NOPE_DIM)
    v = (c_kv @ w_uv).reshape(B, S, N_HEADS, V_HEAD_DIM)
    scale = (QK_NOPE_DIM + QK_ROPE_DIM) ** -0.5
    n_blk = S // Q_BLOCK
    qn_blocks = q_nope.reshape(B, n_blk, Q_BLOCK, N_HEADS, QK_NOPE_DIM).transpose(1, 0, 2, 3, 4)
    qr_blocks = q_rope.reshape(B, n_blk, Q_BLOCK, N_HEADS, QK_ROPE_DIM).transpose(1, 0, 2, 3, 4)

    def attend(blk):
        qn, qr = blk
        s = (jnp.einsum('bqhd,bkhd->bhqk', qn, k_nope, preferred_element_type=jnp.float32)
             + jnp.einsum('bqhr,bkr->bhqk', qr, k_rope, preferred_element_type=jnp.float32))
        p = jax.nn.softmax(s * scale, axis=-1).astype(v.dtype)
        return jnp.einsum('bhqk,bkhd->bqhd', p, v)

    o = lax.map(attend, (qn_blocks, qr_blocks))
    o = o.transpose(1, 0, 2, 3, 4).reshape(B, S, N_HEADS * V_HEAD_DIM)
    return o @ w_o

def encoder_layer(x, ffn1, mix_pre_g, mixer_fn, mixer_params, mix_post_g, ffn2):
    pre1, wg1, wu1, wd1, post1 = ffn1
    x = x + FFN_RESIDUAL_WEIGHT * rms_norm(swiglu(rms_norm(x, pre1), wg1, wu1, wd1), post1)
    x = x + rms_norm(mixer_fn(rms_norm(x, mix_pre_g), *mixer_params), mix_post_g)
    pre2, wg2, wu2, wd2, post2 = ffn2
    x = x + FFN_RESIDUAL_WEIGHT * rms_norm(swiglu(rms_norm(x, pre2), wg2, wu2, wd2), post2)
    return x

def setup_inputs(seed: int = 0) -> dict:
    key = jax.random.key(seed)
    ks = iter(jax.random.split(key, 64))

    def w(shape, fan_in):
        return jax.random.normal(next(ks), shape, jnp.float32) * fan_in ** -0.5

    def g(n):
        return 1.0 + 0.01 * jax.random.normal(next(ks), (n,), jnp.float32)

    def b(n):
        return 0.01 * jax.random.normal(next(ks), (n,), jnp.float32)

    p = {}
    p['x_prompt'] = jax.random.normal(next(ks), (BATCH, SEQ, D_MODEL), jnp.float32)
    p['x_sample'] = jax.random.normal(next(ks), (DEC_BATCH, DEC_SEQ, D_MODEL), jnp.float32)

    def add_ffn(prefix):
        p[prefix + '_pre_g'] = g(D_MODEL)
        p[prefix + '_w_gate'] = w((D_MODEL, D_FF), D_MODEL)
        p[prefix + '_w_up'] = w((D_MODEL, D_FF), D_MODEL)
        p[prefix + '_w_down'] = w((D_FF, D_MODEL), D_FF)
        p[prefix + '_post_g'] = g(D_MODEL)

    add_ffn('l0_ffn1')
    p['l0_mix_pre_g'] = g(D_MODEL)
    p['l0_conv_w_pw1'] = w((D_MODEL, 2 * D_MODEL), D_MODEL)
    p['l0_conv_b_pw1'] = b(2 * D_MODEL)
    p['l0_conv_w_dw'] = w((CONV_WIDTH, D_MODEL), CONV_WIDTH)
    p['l0_conv_b_dw'] = b(D_MODEL)
    p['l0_conv_ln_g'] = g(D_MODEL)
    p['l0_conv_ln_b'] = b(D_MODEL)
    p['l0_conv_w_pw2'] = w((D_MODEL, D_MODEL), D_MODEL)
    p['l0_conv_b_pw2'] = b(D_MODEL)
    p['l0_mix_post_g'] = g(D_MODEL)
    add_ffn('l0_ffn2')
    add_ffn('l1_ffn1')
    p['l1_mix_pre_g'] = g(D_MODEL)
    p['l1_mla_w_dq'] = w((D_MODEL, Q_LORA_RANK), D_MODEL)
    p['l1_mla_q_norm_g'] = g(Q_LORA_RANK)
    p['l1_mla_w_uq'] = w((Q_LORA_RANK, N_HEADS * (QK_NOPE_DIM + QK_ROPE_DIM)), Q_LORA_RANK)
    p['l1_mla_w_dkv'] = w((D_MODEL, KV_LORA_RANK + QK_ROPE_DIM), D_MODEL)
    p['l1_mla_kv_norm_g'] = g(KV_LORA_RANK)
    p['l1_mla_w_uk'] = w((KV_LORA_RANK, N_HEADS * QK_NOPE_DIM), KV_LORA_RANK)
    p['l1_mla_w_uv'] = w((KV_LORA_RANK, N_HEADS * V_HEAD_DIM), KV_LORA_RANK)
    p['l1_mla_w_o'] = w((N_HEADS * V_HEAD_DIM, D_MODEL), N_HEADS * V_HEAD_DIM)
    p['l1_mix_post_g'] = g(D_MODEL)
    add_ffn('l1_ffn2')
    return p

def reference(x_prompt, x_sample,
              l0_ffn1_pre_g, l0_ffn1_w_gate, l0_ffn1_w_up, l0_ffn1_w_down, l0_ffn1_post_g,
              l0_mix_pre_g, l0_conv_w_pw1, l0_conv_b_pw1, l0_conv_w_dw, l0_conv_b_dw,
              l0_conv_ln_g, l0_conv_ln_b, l0_conv_w_pw2, l0_conv_b_pw2, l0_mix_post_g,
              l0_ffn2_pre_g, l0_ffn2_w_gate, l0_ffn2_w_up, l0_ffn2_w_down, l0_ffn2_post_g,
              l1_ffn1_pre_g, l1_ffn1_w_gate, l1_ffn1_w_up, l1_ffn1_w_down, l1_ffn1_post_g,
              l1_mix_pre_g, l1_mla_w_dq, l1_mla_q_norm_g, l1_mla_w_uq, l1_mla_w_dkv,
              l1_mla_kv_norm_g, l1_mla_w_uk, l1_mla_w_uv, l1_mla_w_o, l1_mix_post_g,
              l1_ffn2_pre_g, l1_ffn2_w_gate, l1_ffn2_w_up, l1_ffn2_w_down, l1_ffn2_post_g):
    layers = (
        ((l0_ffn1_pre_g, l0_ffn1_w_gate, l0_ffn1_w_up, l0_ffn1_w_down, l0_ffn1_post_g),
         l0_mix_pre_g,
         (l0_conv_w_pw1, l0_conv_b_pw1, l0_conv_w_dw, l0_conv_b_dw,
          l0_conv_ln_g, l0_conv_ln_b, l0_conv_w_pw2, l0_conv_b_pw2),
         l0_mix_post_g,
         (l0_ffn2_pre_g, l0_ffn2_w_gate, l0_ffn2_w_up, l0_ffn2_w_down, l0_ffn2_post_g)),
        ((l1_ffn1_pre_g, l1_ffn1_w_gate, l1_ffn1_w_up, l1_ffn1_w_down, l1_ffn1_post_g),
         l1_mix_pre_g,
         (l1_mla_w_dq, l1_mla_q_norm_g, l1_mla_w_uq, l1_mla_w_dkv,
          l1_mla_kv_norm_g, l1_mla_w_uk, l1_mla_w_uv, l1_mla_w_o),
         l1_mix_post_g,
         (l1_ffn2_pre_g, l1_ffn2_w_gate, l1_ffn2_w_up, l1_ffn2_w_down, l1_ffn2_post_g)),
    )
    mixers = (conv_module, mla)

    def trunk(x):
        for i in range(DEPTH):
            ffn1, mix_pre_g, mixer_params, mix_post_g, ffn2 = layers[i]
            x = encoder_layer(x, ffn1, mix_pre_g, mixers[i % N_MIXERS], mixer_params, mix_post_g, ffn2)
        return x

    y_prompt = trunk(x_prompt)
    y_sample = trunk(x_sample)
    return (y_prompt, y_sample)


_drawn_inputs = setup_inputs


def setup_inputs(seed=0):
    import zlib

    import numpy as np

    out = dict(_drawn_inputs(seed))
    spreads = {}
    factors = {'l0_ffn1_pre_g': 7.749,
     'l0_ffn1_post_g': 8.0,
     'l0_mix_pre_g': 7.321,
     'l0_conv_b_pw1': 4.33,
     'l0_conv_ln_g': 5.233,
     'l0_conv_ln_b': 4.063,
     'l0_mix_post_g': 7.168,
     'l0_ffn2_pre_g': 8.0,
     'l0_ffn2_post_g': 8.0,
     'l1_ffn1_pre_g': 8.0,
     'l1_ffn1_post_g': 8.0,
     'l1_mix_pre_g': 8.0,
     'l1_mla_q_norm_g': 8.0,
     'l1_mla_kv_norm_g': 8.0,
     'l1_mix_post_g': 64.0,
     'l1_ffn2_pre_g': 64.0,
     'l1_ffn2_post_g': 64.0,
     'l0_conv_b_dw': 4.219,
     'l0_conv_b_pw2': 3.575}
    for name, (base, spread) in spreads.items():
        noise = np.random.default_rng([zlib.crc32(name.encode()), seed]).standard_normal(out[name].shape)
        drawn = base * np.exp(spread * noise) if base else spread * noise
        out[name] = __import__('jax').numpy.asarray(drawn.astype(out[name].dtype))
    for name, factor in factors.items():
        out[name] = (out[name] * factor).astype(out[name].dtype)
    return out
```

```python
from contextlib import ExitStack

import concourse.bass as bass
from concourse import mybir

F32 = mybir.dt.float32
F32R = mybir.dt.float32r
I32 = mybir.dt.int32
ALU = mybir.AluOpType
ACT = mybir.ActivationFunctionType
AX_X = mybir.AxisListType.X

P = 128
D_MODEL = 1024
KT = D_MODEL // P
D_FF = 2816
PROMPT, SAMPLE = 256, 512
TOK = PROMPT + SAMPLE
HALF = TOK // 2
TT = HALF // P
EPS = 1e-6

CHUNKS = D_FF // P
BLOCKS = ((0, 6), (6, 8), (14, 8))
RING = 4
UNIT = KT * P

TAPS = 31
PE_TAPS = 9
DVE_TAPS = TAPS - PE_TAPS
PAD = TAPS // 2
SEG = PROMPT + 2 * PAD
PADDED = SEG + SAMPLE + 2 * PAD
CONV_OUT = PADDED - 2 * PAD

HEADS = 8
NOPE, ROPE, VDIM = 128, 64, 128
Q_RANK, KV_RANK = 384, 256
QT, KVT = Q_RANK // P, KV_RANK // P
PAIRS = HEADS // 2
SCALE = float(NOPE + ROPE) ** -0.5

FFN_UNITS = 2 * CHUNKS + KT * len(BLOCKS)
SUBLAYERS = []
_unit = _up = _out = 0
for _kind in ("ffn", "conv", "ffn", "ffn", "mla", "ffn"):
    _n = {"ffn": (FFN_UNITS, 2 * CHUNKS, 2 * KT * len(BLOCKS)),
          "conv": (3 * KT, 2 * KT, 2 * KT),
          "mla": (2 * QT + 4 * PAIRS + KT, 2 * QT, 2 * KT)}[_kind]
    SUBLAYERS.append((_kind, _unit, _up, _out))
    _unit, _up, _out = _unit + _n[0], _up + _n[1], _out + _n[2]
UNITS = _unit

VEC = {}
_col = 0
for _name, _n in ([(f"pre{i}", KT) for i in range(6)] + [(f"post{i}", KT) for i in range(6)]
                  + [("b_pw1", 2 * KT), ("b_dw", KT), ("ln_g", KT), ("ln_b", KT), ("b_pw2", KT),
                     ("w_dw", KT * TAPS), ("q_g", QT), ("kv_g", KVT)]):
    VEC[_name] = _col
    _col += _n
VECS = _col


CREDIT = 2
SCORE_BUFS = 3


def at(start, count=1):
    return bass.ds(start, count)


def trunk(nc, x_in, weights, vectors, rope_in, ident_in, y_out, stages=len(SUBLAYERS)):
    with ExitStack() as ctx:
        place, spot = [(nc.sbuf_base + 31) // 32 * 32], {}

        def sbuf(name, shape, dt=F32):
            size = 4
            for n in shape[1:]:
                size *= n
            spot[name] = place[0]
            place[0] += (size + 31) // 32 * 32
            return nc.alloc_sbuf_tensor_at(name, shape, dt, offset=spot[name])

        def over(name, shape, offset, dt=F32):
            return nc.alloc_sbuf_tensor_at(name, shape, dt, offset=offset)

        def sem(name):
            return ctx.enter_context(nc.semaphore(name))

        x = sbuf("x", [P, KT, TOK])
        xg = sbuf("xg", [P, 2, KT, TOK], F32R)
        h = sbuf("h", [P, 2, KT, TOK], F32R)
        y = sbuf("y", [P, KT, TOK])
        w_ring = sbuf("w_ring", [P, RING, 2, UNIT], F32R)
        w_stage = sbuf("w_stage", [P, RING, UNIT])
        vec = sbuf("vec", [P, VECS])
        half_post = sbuf("half_post", [P, 6 * KT])
        gu = sbuf("gu", [P, 2, 2, HALF])
        act_out = sbuf("act_out", [P, 2, HALF])
        prod = sbuf("prod", [P, 2, HALF])
        sq = sbuf("sq", [P, 2, HALF])
        acc = sbuf("acc", [P, 2, HALF])
        pre_acc = sbuf("pre_acc", [P, HALF])
        r_post = sbuf("r_post", [P, 2, HALF])
        r_pre = sbuf("r_pre", [P, 2, HALF])
        mean_w = sbuf("mean_w", [P, P])
        ones_w = sbuf("ones_w", [P, P])
        ident = sbuf("ident", [P, P])
        diag = sbuf("diag", [P, TT, P])
        newton = sbuf("newton", [P, 4, 4 * TT])
        soft = sbuf("soft", [P, 4, SCORE_BUFS])
        carrier = sbuf("carrier", [P, 4])
        zero = sbuf("zero", [P, 1])
        assert place[0] <= nc.sbuf_usable_end, place[0] - nc.sbuf_usable_end

        cin = over("cin", [P, 2, PADDED], spot["h"])
        cacc = over("cacc", [P, 2, CONV_OUT], spot["h"] + 2 * PADDED * 4)
        ln_diag = over("ln_diag", [P, 2, TT, P], spot["h"])
        tap_w = over("tap_w", [P, 2, PE_TAPS, P], spot["h"] + (2 * PADDED + 2 * CONV_OUT + 7) * 4 // 32 * 32)
        KV0, KR = QT, QT + KVT
        v_r = over("v_r", [P, 2, TOK // P, 2 * VDIM], spot["y"], F32R)
        qn_r = over("qn_r", [P, 2, 2, TOK], spot["y"] + TOK // P * 2 * VDIM * 8, F32R)
        kn_r = over("kn_r", [P, 2, 2, TOK], spot["x"], F32R)
        KEYS = SAMPLE // P
        pt_a = [over(f"pt_a{i}", [P, KEYS, 256], spot["x"] + 2 * TOK * 8 + i * KEYS * 1024, F32R) for i in range(2)]
        pt_b = [over(f"pt_b{i}", [P, KEYS, 256], spot["h"] + (i * KT + 6) * TOK * 4, F32R) for i in range(2)]
        pt = [pt_a, pt_b]
        qr_r = over("qr_r", [P, 2, TOK], spot["sq"], F32R)
        rope_tmp = over("rope_tmp", [P, 4, HALF], spot["act_out"])
        table = over("table", [P, 2, TOK], spot["r_post"])
        probs = over("probs", [P, SCORE_BUFS, SAMPLE], spot["gu"])
        lat_diag = over("lat_diag", [P, 4, TT, P], spot["act_out"])

        ps = ctx.enter_context(nc.psum_tensor("ps", [P, 8, 512], F32))
        OUT_BANK, SPREAD_BANK, SUM_BANK = 4, 6, 7
        SCORE_BANKS = (4, 5, 3)
        LAT_BANKS = (0, 1, 4, 5)
        x_kept = nc.dram_tensor("x_kept", (P, KT, TOK), F32, kind="Internal").ap()

        x_loaded, vec_loaded, ident_loaded = sem("x_loaded"), sem("vec_loaded"), sem("ident_loaded")
        w_loaded = [sem(f"w_loaded{s}") for s in range(RING)]
        mean_ready, consts = sem("mean_ready"), sem("consts")
        w_hi, w_split, w_used = sem("w_hi"), sem("w_split"), sem("w_used")
        up_full, scaled, act_done, prod_done = sem("up_full"), sem("scaled"), sem("act_done"), sem("prod_done")
        h_hi, h_done = sem("h_hi"), sem("h_done")
        out_full, y_done, sq_done, acc_done = sem("out_full"), sem("y_done"), sem("sq_done"), sem("acc_done")
        sums_full, sums_read, newton_step = sem("sums_full"), sem("sums_read"), sem("newton_step")
        diag_ready, spread_full, rms_done = sem("diag_ready"), sem("spread_full"), sem("rms_done")
        t_ready, x_done, xg_hi, xg_done = sem("t_ready"), sem("x_done"), sem("xg_hi"), sem("xg_done")
        pre_sq, pre_sq_used, pre_sums_full = sem("pre_sq"), sem("pre_sq_used"), sem("pre_sums_full")
        pads, conv_in, tap_done, conv_done = sem("pads"), sem("conv_in"), sem("tap_done"), sem("conv_done")
        tap_w_ready, taps_full, chains_done = sem("tap_w_ready"), sem("taps_full"), sem("chains_done")
        mean_full, centred, dev_sq = sem("mean_full"), sem("centred"), sem("dev_sq")
        dev_sq_used = sem("dev_sq_used")
        ln_done, ln_act, ln_hi, ln_split = sem("ln_done"), sem("ln_act"), sem("ln_hi"), sem("ln_split")
        x_saved, x_back, table_loaded = sem("x_saved"), sem("x_back"), sem("table_loaded")
        lat_sq, lat_f = sem("lat_sq"), sem("lat_f")
        proj_full, part_hi, part_done = sem("proj_full"), sem("part_hi"), sem("part_done")
        swapped, rope_part, rotated = sem("swapped"), sem("rope_part"), sem("rotated")
        s_full, s_max, s_nmax, s_exp, s_inv, p_done = (
            sem(n) for n in ("s_full", "s_max", "s_nmax", "s_exp", "s_inv", "p_done"))
        tr_full, pt_hi, pt_done = sem("tr_full"), sem("pt_hi"), sem("pt_done")
        pv_full, o_hi, o_done = sem("pv_full"), sem("o_hi"), sem("o_done")
        stored = sem("stored")

        todo = SUBLAYERS[:stages]
        units = SUBLAYERS[stages][1] if stages < len(SUBLAYERS) else UNITS

        def cols(half):
            return slice(half * HALF, (half + 1) * HALF)

        def v(name, k):
            return vec[:, at(VEC[name] + k)]

        def step(b, half, k):
            return (b * 2 + half) * KT + k

        def ffn_items(b):
            return 2 * CHUNKS * sum(kind == "ffn" for kind, *_ in SUBLAYERS[:b])

        def act_items(b):
            return ffn_items(b) + 2 * KT * (b > 1)

        def norm(b, what, half=0):
            base = 4 * b + 2 * (b > 1) + 4 * (b > 4)
            return base + half + {"pre": 0, "inner": 2, "post": 2 + 2 * (b == 1) + 4 * (b == 4)}[what]

        STARTING = ((0, 0), (1, 0), (0, 1), (1, 1))
        STEADY = ((0, 0), (0, 1), (1, 0), (1, 1))
        START_BANKS = (0, 2, OUT_BANK, 2)
        STEADY_BANKS = (0, 2, 0, 2)
        OUTS = tuple((m, half) for m in range(KT) for half in range(2))
        LAST_OUTS = OUTS[:8] + tuple((m, half) for half in range(2) for m in range(KT // 2, KT))

        def square_place(half, k):
            if half == 0 and k < 4:
                return gu[:, k // 2, k % 2, :]
            if half == 0 and k < 6:
                return act_out[:, k - 4, :]
            return sq[:, k % 2, :]

        DEV_SQ = [gu[:, 0, 0, :], gu[:, 0, 1, :], gu[:, 1, 0, :], gu[:, 1, 1, :], sq[:, 0, :], sq[:, 1, :]]
        Q_TILES = [(i // 6, (i % 6) * P, (0, PROMPT) if i % 6 < 2 else (PROMPT, SAMPLE)) for i in range(12)]
        LAT_SQ = [gu[:, 0, 0, :], gu[:, 0, 1, :], gu[:, 1, 0, :], gu[:, 1, 1, :], act_out[:, 0, :],
                  act_out[:, 1, :], prod[:, 0, :], prod[:, 1, :], sq[:, 0, :], sq[:, 1, :]]
        LATENTS = QT + KVT
        LAT_PARTS = 2 * (LATENTS + 1)
        PROJ = 13

        block = ctx.enter_context(nc.Block())

        @block.sync
        def _(sp):
            sp.dma_start(vec[:, :], vectors).then_inc(vec_loaded, 16)
            for s in range(RING):
                sp.dma_start(w_stage[:, s, :], weights[s]).then_inc(w_loaded[s], 16)
                if s == 0:
                    sp.dma_start(x[:, :, :], x_in).then_inc(x_loaded, 16)
            sp.dma_start(ident[:, :], ident_in).then_inc(ident_loaded, 16)

            def load(u, s):
                sp.wait_ge(w_split, u - (RING - 1))
                sp.dma_start(w_stage[:, at(s), :], weights[at(u), :, :].rearrange("a p n -> p a n")
                             ).then_inc(w_loaded[s], 16)

            full = units // RING
            with sp.Fori(1, full) as i:
                for s in range(RING):
                    load(i * RING + s, s)
            for u in range(full * RING, units):
                load(u, u % RING)
            for half in range(2):
                sp.wait_ge(x_done, step(stages - 1, half, KT - 1) + 1)
                sp.dma_start(y_out[:, :, cols(half)], x[:, :, cols(half)]).then_inc(stored, 16)
            sp.wait_ge(stored, 32)

        @block.gpsimd
        def _(pool):
            pool.memset(ones_w[:, :], 1.0).then_inc(mean_ready, 1)
            pool.memset(zero[:, :], 0.0).then_inc(mean_ready, 1)
            pool.memset(mean_w[:, :], 1.0 / D_MODEL).then_inc(mean_ready, 1)
            pool.wait_ge(mean_ready, 2)

            def split(u, s, loads):
                pool.wait_ge(w_loaded[s], 16 * loads)
                if not isinstance(u, int) or u >= RING:
                    pool.wait_ge(w_used, u - (RING - 1))
                pool.tensor_tensor(w_ring[:, s, 0, :], w_stage[:, s, :], zero[:, 0:1].broadcast_to([P, UNIT]),
                                   ALU.add).then_inc(w_hi, 1)
                pool.wait_ge(w_hi, u + 1)
                pool.tensor_tensor(w_ring[:, s, 1, :], w_stage[:, s, :], w_ring[:, s, 0, :].bitcast(F32),
                                   ALU.subtract).then_inc(w_split, 1)

            def sum_squares(b, half):
                for k in range(1, KT):
                    pool.wait_ge(pre_sq, step(b, half, k) + 1)
                    one = square_place(half, 0) if k == 1 else pre_acc[:, :]
                    if k == 1 and b + half > 0:
                        pool.wait_ge(pre_sums_full, 2 * b + half)
                    if k > 1:
                        pool.wait_ge(pre_sq_used, step(b, half, k))
                    pool.tensor_tensor(pre_acc[:, :], one, square_place(half, k), ALU.add
                                       ).then_inc(pre_sq_used, 2 if k == 1 else 1)

            for s in range(RING):
                split(s, s, 1)
            for b, (_, unit, _, _) in enumerate(todo):
                for half in range(2):
                    sum_squares(b, half)
                lo = unit + RING
                hi = min(SUBLAYERS[b + 1][1] + RING if b + 1 < len(SUBLAYERS) else units, units)
                with pool.Fori(0, (hi - lo) // RING) as i:
                    for s in range(RING):
                        split(i * RING + (lo + s), (lo + s) % RING, i + ((lo + s) // RING + 1))
                for u in range(lo + (hi - lo) // RING * RING, hi):
                    split(u, u % RING, u // RING + 1)

        @block.tensor
        def _(pe):
            def mm3(out, w, v, start, stop, release=False):
                mm = pe.matmul(out, w[0], v[0], start=start, stop=False)
                if release:
                    mm.then_inc(w_used, 1)
                pe.matmul(out, w[1], v[0], start=False, stop=False)
                return pe.matmul(out, w[0], v[1], start=False, stop=stop)

            def tile(s, t, n=P):
                return [w_ring[:, s % RING, i, t * P:t * P + n] for i in range(2)]

            def both(t, k, c):
                return [t[:, i, k, c] for i in range(2)]

            def sums(bank, c0, squares, first, last):
                for c in range(TT):
                    mm = pe.matmul(ps[:, bank, c0 + c:c0 + c + 1], squares[:, c * P:(c + 1) * P], ones_w[:, 0:1],
                                   start=first and c == 0, stop=last, skip_group_check=True)
                return mm

            def spread(no, bank=SPREAD_BANK, d=None):
                pe.wait_ge(diag_ready, no + 1)
                pe.matmul(ps[:, bank, 0:HALF], ones_w[:, :], (diag[:, :, :] if d is None else d
                          ).rearrange("p a n -> p (a n)"), start=True, stop=True).then_inc(spread_full, 1)

            def pre_square(b, half):
                pe.wait_ge(pre_sq_used, step(b, half, KT - 1) + 1)
                if half == 1:
                    pe.wait_ge(sums_read, norm(b, "pre") + 1)
                sums(SUM_BANK, 0, pre_acc[:, :], True, True).then_inc(pre_sums_full, 1)

            def post_square(b, half):
                pe.wait_ge(acc_done, 2 * b + half + 1)
                sums(SPREAD_BANK, 0, acc[:, half, :], True, True).then_inc(sums_full, 1)

            def up_item(q, bank, s, half, release, starting=None, n=None):
                for k in range(KT):
                    if starting is not None and n == 2 and k == KT // 2:
                        spread(norm(starting, "pre", 0))
                    if starting is not None and n == 3 and k == KT - 3:
                        pre_square(starting, 1)
                    if starting is not None and n in (0, 2):
                        pe.wait_ge(xg_done, step(starting, half, k) + 1)
                    for g in range(2):
                        mm = mm3(ps[:, bank + g, 0:HALF], tile(s + g, k), both(xg, k, cols(half)),
                                 k == 0, k == KT - 1, release=release and k == 0 and g == 0)
                        if half == 1 and k == KT - 1 and g == 0:
                            mm.then_inc(w_used, 1)
                    if starting is not None and starting > 0 and (n, k) == (0, KT - 1):
                        post_square(starting - 1, 1)
                    if starting is not None and starting > 0 and (n, k) == (1, KT // 2 - 1):
                        spread(norm(starting - 1, "post", 1))
                    if starting is not None and (n, k) == (1, KT - 3):
                        pre_square(starting, 0)
                mm.then_inc(up_full, 1)
                if starting is not None and n == 3:
                    spread(norm(starting, "pre", 1))

            def up_start(b, unit, q):
                for n, (j, half) in enumerate(STARTING):
                    pe.wait_ge(w_split, unit + 2 * j + 2)
                    if n == 2:
                        pe.wait_ge(y_done, SUBLAYERS[b][3] + CREDIT)
                    elif q + n >= 2:
                        pe.wait_ge(scaled, q + n - 1)
                    up_item(q + n, START_BANKS[n], unit + 2 * j, half, n == 3 or (n == 0 and b > 0),
                            starting=b, n=n)

            def up_pair(q, unit, s, items=(0, 1, 2, 3)):
                for n in items:
                    j, half = STEADY[n]
                    if half == 0:
                        pe.wait_ge(w_split, unit + (2 * j + 2))
                    pe.wait_ge(scaled, q + (n - 1))
                    up_item(q, STEADY_BANKS[n], s + 2 * j, half, half == 0)

            def out_items(d, unit, s, src, nk, outs, release_first=True, need=None, each=None,
                          last_of=None):
                m0 = outs[0][0]
                for n, (m, half) in enumerate(outs):
                    pe.wait_ge(w_split, unit + (m - m0 + 1))
                    pe.wait_ge(y_done, d + (n - 1 + CREDIT))
                    if need is not None and n < 2:
                        pe.wait_ge(*need[n])
                    release = (n > 0 and outs[n - 1][1] == 1) or (n == 0 and release_first)
                    for k in range(nk):
                        if each is not None and n < 2:
                            pe.wait_ge(each, n * nk + k + 1)
                        mm = mm3(ps[:, OUT_BANK + n % 2, 0:HALF], tile(s + m - m0, k), both(src, k, cols(half)),
                                 k == 0, k == nk - 1, release=release and k == 0)
                        if last_of is not None and (n, k) == (12, nk // 2):
                            post_square(last_of, 0)
                        if last_of is not None and (n, k) == (13, nk // 2):
                            spread(norm(last_of, "post", 0))
                    mm.then_inc(out_full, 1)

            def conv_taps(c, slot):
                pe.wait_ge(conv_in, 5 if isinstance(c, int) and c == 0 else c * 3 + 3)
                pe.wait_ge(tap_w_ready, c + 1)
                if not isinstance(c, int) or c > 0:
                    pe.wait_ge(conv_done, c)
                for i in range(PE_TAPS):
                    for bank, t, n in ((OUT_BANK, 0, PROMPT), (OUT_BANK + 1, SEG, SAMPLE)):
                        mm = pe.matmul(ps[:, bank, 0:n], tap_w[:, slot, i, :],
                                       cin[:, slot, t + DVE_TAPS + i:t + DVE_TAPS + i + n],
                                       start=i == 0, stop=i == PE_TAPS - 1)
                mm.then_inc(taps_full, 1)

            def mean(c, last=False):
                pe.wait_ge(conv_done, c + 1)
                for half in range(2):
                    mm = pe.matmul(ps[:, SPREAD_BANK + half:SPREAD_BANK + half + 1, 0:HALF], mean_w[:, :],
                                   y[:, at(c), cols(half)], start=False, stop=last)
                return mm

            def attention(b, unit):
                up_q = SUBLAYERS[b][2] + 4
                for n in range(2):
                    pe.wait_ge(w_split, unit + 6)
                    pe.wait_ge(scaled, up_q + n - 1)
                    up_item(up_q + n, STEADY_BANKS[n], unit + 4, n, n == 0)
                pe.wait_ge(lat_sq, 2 * LATENTS)
                for g in range(4):
                    tiles = range(QT) if g < 2 else range(QT, LATENTS)
                    for t in tiles:
                        mm = sums(SUM_BANK, g * TT, LAT_SQ[2 * t + g % 2], t == tiles[0], t == tiles[-1])
                        if g == 0 and t == 0:
                            mm.then_inc(w_used, 1)
                    mm.then_inc(sums_full, 1)
                for g in range(4):
                    spread(norm(b, "inner") + g, LAT_BANKS[g], lat_diag[:, g, :, :])

                with pe.Fori(0, PAIRS) as p:
                    base = unit + 2 * QT
                    s = base % RING
                    for n in range(PROJ):
                        if n == 0:
                            pe.wait_ge(part_done, 2 * QT)
                            pe.wait_ge(o_done, p * 6)
                        elif n > 3:
                            pe.wait_ge(part_done, p * PROJ + (LAT_PARTS + n - 3))
                        bank = n % 4
                        if n in (0, 4, 6, 10):
                            pe.wait_ge(w_split, p * 4 + (base + (0, 4, 6, 10).index(n) + 1))
                        rel = n in (4, 6, 10)
                        if n < 4:
                            for k in range(QT):
                                mm = mm3(ps[:, bank, 0:HALF], tile(s, (n // 2) * QT + k), both(h, k, cols(n % 2)),
                                         k == 0, k == QT - 1)
                        elif n < 6:
                            for k in range(QT):
                                mm = mm3(ps[:, bank, 0:HALF], tile(s + 1, k), both(h, k, cols(n % 2)),
                                         k == 0, k == QT - 1, release=rel and k == 0)
                        elif n < 10:
                            for k in range(KVT):
                                mm = mm3(ps[:, bank, 0:HALF], tile(s + 2, (n - 6) // 2 * KVT + k),
                                         both(h, KV0 + k, cols(n % 2)), k == 0, k == KVT - 1,
                                         release=rel and k == 0)
                        else:
                            for i in range(2):
                                t = (n - 10) * 2 + i
                                for k in range(KVT):
                                    mm = mm3(ps[:, bank, i * 256:(i + 1) * 256],
                                             both(h, KV0 + k, slice(t * P, (t + 1) * P)),
                                             tile(s + 3, 2 * k, 256), k == 0, k == KVT - 1,
                                             release=rel and k == 0 and i == 0)
                        mm.then_inc(proj_full, 1)

                    def scores(i):
                        head, q0, (k0, nk) = Q_TILES[i]
                        if i == 0:
                            pe.wait_ge(part_done, p * PROJ + (LAT_PARTS + PROJ))
                        pe.wait_ge(s_exp, p * 12 + max(i - 2, 0))
                        out = ps[:, SCORE_BANKS[i % SCORE_BUFS], 0:nk]
                        qs, ks = slice(q0, q0 + P), slice(k0, k0 + nk)
                        mm3(out, both(qn_r, head, qs), both(kn_r, head, ks), True, False, release=(i == 0))
                        r = slice(head * ROPE, (head + 1) * ROPE)
                        mm3(out, [qr_r[r, j, qs] for j in range(2)], [h[r, j, KR, ks] for j in range(2)],
                            False, True).then_inc(s_full, 1)

                    def transposes(i):
                        head, q0, (k0, nk) = Q_TILES[i]
                        pe.wait_ge(p_done, p * 12 + (i + 1))
                        if i % 2 == 0:
                            pe.wait_ge(pt_done, p * 6 + i // 2)
                        for t in range(nk // P):
                            c = (t % 2) * 256 + (i % 2) * P
                            mm = pe.transpose(ps[:, 6 + t // 2, c:c + P], probs[:, i % SCORE_BUFS, t * P:(t + 1) * P],
                                              ident[:, :])
                        mm.then_inc(tr_full, 1)

                    def values(j):
                        head, q0, (k0, nk) = Q_TILES[2 * j]
                        pe.wait_ge(pt_done, p * 6 + (j + 1))
                        if j >= 2:
                            pe.wait_ge(o_done, p * 6 + (j - 1))
                        for t in range(nk // P):
                            mm = mm3(ps[:, j % 2, 0:256],
                                     [v_r[:, i, k0 // P + t, head * VDIM:(head + 1) * VDIM] for i in range(2)],
                                     [pt[j % 2][i][:, t, :] for i in range(2)], t == 0, t == nk // P - 1)
                        mm.then_inc(pv_full, 1)

                    for i in range(16):
                        if i < 12:
                            scores(i)
                        if 2 <= i < 14:
                            transposes(i - 2)
                        if i >= 5 and i % 2 == 1:
                            values((i - 5) // 2)

            pe.wait_ge(mean_ready, 3)
            pe.wait_ge(ident_loaded, 16)
            for b, (kind, unit, q, d) in enumerate(todo):
                up_start(b, unit, q)
                if kind == "ffn":
                    for n, (c0, nc_) in enumerate(BLOCKS):
                        ub, qb, db = unit + 2 * c0 + KT * n, q + 2 * c0, d + 2 * KT * n
                        with pe.Fori(1 if n == 0 else 0, nc_ // 2) as i:
                            up_pair(i * 4 + qb, i * 4 + ub, ub)
                        made = ffn_items(b) + 2 * (c0 + nc_)
                        need = ((h_done, made - 1), (h_done, made))
                        ub += 2 * nc_
                        if n < len(BLOCKS) - 1:
                            with pe.Fori(0, KT // 4) as i:
                                out_items(i * 8 + db, i * 4 + ub, ub, h, nc_, OUTS[:8], need=need)
                        else:
                            out_items(db, ub, ub, h, nc_, LAST_OUTS, need=need, last_of=b)
                elif kind == "conv":
                    conv_taps(0, 0)
                    for half in range(2):
                        pe.matmul(ps[:, SPREAD_BANK + half, 0:HALF], mean_w[:, :],
                                  zero[:, 0:1].broadcast_to([P, HALF]), start=True, stop=False)
                    with pe.Fori(1, KT // 2) as i:
                        for j in range(2):
                            up_pair(i * 4 + q, i * 4 + unit, unit, (2 * j, 2 * j + 1))
                            conv_taps(i * 2 + (j - 1), 1 - j)
                            mean(i * 2 + (j - 2))
                    conv_taps(KT - 1, 1)
                    mean(KT - 2)
                    mean(KT - 1, last=True).then_inc(mean_full, 1)
                    for half in range(2):
                        for k in range(KT):
                            pe.wait_ge(dev_sq, half * KT + k + 1)
                            sums(OUT_BANK + half, 0, DEV_SQ[(half * KT + k) % len(DEV_SQ)], k == 0, k == KT - 1
                                 ).then_inc(dev_sq_used, 1)
                    for half in range(2):
                        spread(norm(b, "inner", half), SPREAD_BANK + half, ln_diag[:, half, :, :])
                    ub = unit + 2 * KT
                    out_items(d, ub, ub, xg, KT, LAST_OUTS, each=ln_split, last_of=b)
                else:
                    attention(b, unit)
                    pe.wait_ge(o_done, 6 * PAIRS)
                    ub = unit + 2 * QT + 4 * PAIRS
                    out_items(d, ub, ub, xg, KT, LAST_OUTS, release_first=False, last_of=b)
            post_square(stages - 1, 1)
            spread(norm(stages - 1, "post", 1))

        @block.scalar
        def _(act):
            def input_hi(b, half, k):
                if b == 0:
                    act.wait_ge(x_loaded, 16)
                else:
                    act.wait_ge(x_done, step(b - 1, half, k) + 1)
                act.activation(xg[:, 0, k, cols(half)], x[:, k, cols(half)], ACT.Copy,
                               scale=v(f"pre{b}", k)).then_inc(xg_hi, 1)

            def input_square(b, half, k):
                if half == 1:
                    act.wait_ge(pre_sq_used, step(b, half, k) - 1)
                act.activation(square_place(half, k), x[:, k, cols(half)], ACT.Square).then_inc(pre_sq, 1)

            def output_square(d, n, m, half):
                act.wait_ge(y_done, d + (n + 1 + CREDIT))
                act.activation(sq[:, n % 2, :], y[:, m, cols(half)], ACT.Square).then_inc(sq_done, 1)

            def ffn_item(q, g, par, c, half):
                act.wait_ge(scaled, q + 1)
                act.activation(act_out[:, par, :], gu[:, par, 0, :], ACT.Silu).then_inc(act_done, 1)
                act.wait_ge(prod_done, g + 1)
                act.activation(h[:, 0, at(c), cols(half)], prod[:, par:par + 1, :], ACT.Copy).then_inc(h_hi, 1)

            def conv_item(q, par, c):
                act.wait_ge(scaled, q + 1)
                act.activation(carrier[:, par:1 + par], gu[:, par, 1, 0:1], ACT.Copy)
                act.activation(act_out[:, par, :], gu[:, par, 1, :], ACT.Sigmoid,
                               bias=v("b_pw1", c + KT)).then_inc(act_done, 1)

            def tap_weights(c, slot):
                if not isinstance(c, int) or c >= 2:
                    act.wait_ge(taps_full, c - 1)
                act.activation(carrier[:, 2 + slot:3 + slot], ident[:, 0:1], ACT.Copy)
                for i in range(PE_TAPS):
                    ins = act.activation(tap_w[:, slot, i, :], ident[:, :], ACT.Copy,
                                         scale=v("w_dw", c * TAPS + (DVE_TAPS + i)))
                ins.then_inc(tap_w_ready, 1)

            def start(b, d):
                for k in range(KT - 2):
                    if b > 0 and k == KT // 2:
                        output_square(d, 14, *LAST_OUTS[14])
                    input_hi(b, 0, k)
                    input_square(b, 0, k)
                for k in (KT - 2, KT - 1):
                    input_hi(b, 0, k)
                if b > 0:
                    output_square(d, 15, *LAST_OUTS[15])
                    act.wait_ge(acc_done, 2 * b)
                for k in (KT - 2, KT - 1):
                    input_square(b, 0, k)
                for k in range(4):
                    input_hi(b, 1, k)
                for k in range(KT):
                    input_square(b, 1, k)
                    if 1 <= k < 5:
                        input_hi(b, 1, k + 3)

            def swap(src, half):
                for g in range(4):
                    to = g ^ 1
                    ins = act.activation(rope_tmp[32 * to:32 * to + 32, 0, :], src[32 * g:32 * g + 32],
                                         ACT.Copy)
                ins.then_inc(swapped, 1)

            def attention(b, q):
                act.wait_ge(x_done, step(b, 0, 0))
                act.dma_start(x_kept, x[:, :, :]).then_inc(x_saved, 16)
                act.wait_ge(pre_sq_used, step(b, 1, KT - 1) + 1)
                for n, (j, half) in enumerate(STARTING + ((2, 0), (2, 1))):
                    act.wait_ge(scaled, q + n + 1)
                    for t in (2 * j, 2 * j + 1):
                        if t < LATENTS:
                            act.activation(LAT_SQ[2 * t + half], y[:, t, cols(half)], ACT.Square
                                           ).then_inc(lat_sq, 1)
                act.dma_start(table[:, :, :], rope_in).then_inc(table_loaded, 16)
                for n in range(2 * LATENTS):
                    act.wait_ge(lat_f, n + 1)
                    act.activation(h[:, 0, n // 2, cols(n % 2)], prod[:, n % 2, :], ACT.Copy).then_inc(part_hi, 1)
                act.wait_ge(part_done, 2 * LATENTS)
                for half in range(2):
                    if half == 1:
                        act.wait_ge(part_done, 2 * LATENTS + 1)
                    swap(y[:, KR, cols(half)], half)
                    act.wait_ge(rotated, half + 1)
                    act.activation(h[:, 0, KR, cols(half)], rope_tmp[:, 3, :], ACT.Copy).then_inc(part_hi, 1)
                act.wait_ge(x_saved, 16)
                with act.Fori(0, PAIRS) as p:
                    for n in range(PROJ):
                        act.wait_ge(proj_full, p * PROJ + (n + 1))
                        bank, half = n % 4, n % 2
                        if n < 4:
                            act.activation(qn_r[:, 0, n // 2, cols(half)], ps[:, bank, 0:HALF], ACT.Copy
                                           ).then_inc(part_hi, 1)
                        elif n < 6:
                            act.wait_ge(part_done, p * PROJ + (LAT_PARTS + n))
                            swap(ps[:, bank, 0:HALF], half)
                            act.wait_ge(rotated, p * 2 + (n - 4 + 3))
                            act.activation(qr_r[:, 0, cols(half)], rope_tmp[:, 3, :], ACT.Copy).then_inc(part_hi, 1)
                        elif n < 10:
                            act.activation(kn_r[:, 0, (n - 6) // 2, cols(half)], ps[:, bank, 0:HALF], ACT.Copy
                                           ).then_inc(part_hi, 1)
                        else:
                            t = (n - 10) * 2
                            act.activation(v_r[:, 0, t:t + 2, :],
                                           ps[:, bank, :].rearrange("p (a n) -> p a n", a=2), ACT.Copy
                                           ).then_inc(part_hi, 1)

                    def expo(i):
                        nk = Q_TILES[i][2][1]
                        act.wait_ge(s_nmax, p * 12 + (i + 1))
                        act.wait_ge(tr_full, p * 12 + max(i - 2, 0))
                        s = i % SCORE_BUFS
                        act.activation(probs[:, s, 0:nk], ps[:, SCORE_BANKS[s], 0:nk], ACT.Exp,
                                       bias=soft[:, 1, s:s + 1], scale=SCALE,
                                       accum_out=soft[:, 2, s:s + 1]).then_inc(s_exp, 1)

                    def turned(j):
                        nk = Q_TILES[2 * j][2][1]
                        act.wait_ge(tr_full, p * 12 + (2 * j + 2))
                        act.wait_ge(pv_full, p * 6 + max(j - 1, 0))
                        for g in range(nk // 256):
                            ins = act.activation(pt[j % 2][0][:, 2 * g:2 * g + 2, :],
                                                 ps[:, 6 + g, :].rearrange("p (a n) -> p a n", a=2), ACT.Copy)
                        ins.then_inc(pt_hi, 1)

                    def output(j):
                        head, q0, _ = Q_TILES[2 * j]
                        act.wait_ge(pv_full, p * 6 + (j + 1))
                        act.activation(xg[:, 0, at(p * 2 + head), q0:q0 + 256], ps[:, j % 2:j % 2 + 1, 0:256],
                                       ACT.Copy).then_inc(o_hi, 1)

                    for i in range(17):
                        if i < 12:
                            expo(i)
                        if i >= 3 and i % 2 == 1 and i < 15:
                            turned((i - 3) // 2)
                        if i >= 6 and i % 2 == 0:
                            output((i - 6) // 2)
                act.wait_ge(o_done, 6 * PAIRS)
                act.dma_start(x[:, :, :], x_kept).then_inc(x_back, 16)

            act.wait_ge(vec_loaded, 16)
            start(0, 0)
            for b, (kind, unit, q, d) in enumerate(todo):
                g = ffn_items(b)
                if kind == "ffn":
                    for n, (c0, nc_) in enumerate(BLOCKS):
                        qb, gb = q + 2 * c0, g + 2 * c0
                        if n == 0:
                            for m, (j, half) in enumerate(STARTING):
                                ffn_item(qb + m, gb + m, m % 2, j, half)
                        with act.Fori(1 if n == 0 else 0, nc_ // 2) as i:
                            for m, (j, half) in enumerate(STEADY):
                                ffn_item(i * 4 + (qb + m), i * 4 + (gb + m), m % 2, i * 2 + j, half)
                    d += 2 * KT * (len(BLOCKS) - 1)
                elif kind == "conv":
                    for c in range(2):
                        tap_weights(c, c)
                    for m, (j, half) in enumerate(STARTING):
                        conv_item(q + m, m % 2, j)
                    with act.Fori(1, KT // 2) as i:
                        for m, (j, half) in enumerate(STEADY):
                            conv_item(i * 4 + (q + m), m % 2, i * 2 + j)
                            if half == 1:
                                tap_weights(i * 2 + j, j)
                    for n in range(2 * KT):
                        half, k = n // KT, n % KT
                        act.wait_ge(centred, n + 1)
                        if n >= len(DEV_SQ):
                            act.wait_ge(dev_sq_used, n + 1 - len(DEV_SQ))
                        act.activation(DEV_SQ[n % len(DEV_SQ)], y[:, k, cols(half)], ACT.Square).then_inc(dev_sq, 1)
                    for n in range(2 * KT):
                        half, k = n // KT, n % KT
                        act.wait_ge(ln_done, n + 1)
                        if n >= 2:
                            act.wait_ge(ln_split, n - 1)
                        act.activation(act_out[:, k % 2, :], prod[:, k % 2, :], ACT.Silu,
                                       bias=v("ln_b", k)).then_inc(ln_act, 1)
                        act.wait_ge(ln_act, n + 1)
                        act.activation(xg[:, 0, k, cols(half)], act_out[:, k % 2, :], ACT.Copy).then_inc(ln_hi, 1)
                else:
                    attention(b, q)
                for n, (m, half) in enumerate(LAST_OUTS[:14]):
                    output_square(d, n, m, half)
                if b + 1 < stages:
                    start(b + 1, d)
                else:
                    output_square(d, 14, *LAST_OUTS[14])
                    output_square(d, 15, *LAST_OUTS[15])

        @block.vector
        def _(dve):
            steps = [0]

            def stepped(ins):
                steps[0] += 1
                ins.then_inc(newton_step, 1)
                dve.wait_ge(newton_step, steps[0])

            def read_sums(src, c0, n, count):
                dve.tensor_scalar(newton[:, 0, c0:c0 + n], src, 1.0 / count, EPS, ALU.mult, ALU.add
                                  ).then_inc(sums_read, 1)

            def inverse_root(n):
                v_, r, a, b_ = (newton[:, i, 0:n] for i in range(4))
                stepped(dve.tensor_scalar(a.bitcast(I32), v_.bitcast(I32), 1, None, ALU.logical_shift_right))
                stepped(dve.tensor_scalar(r.bitcast(I32), a.bitcast(I32), -1.0, float(0x5F3759DF),
                                          ALU.mult, ALU.add))
                for _ in range(3):
                    stepped(dve.scalar_tensor_tensor(a, r, -0.5, r, ALU.mult, ALU.mult))
                    stepped(dve.tensor_tensor(b_, a, v_, ALU.mult))
                    stepped(dve.scalar_tensor_tensor(r, b_, 1.5, r, ALU.add, ALU.mult))

            def diagonals(to, c0):
                for c in range(TT):
                    ins = dve.tensor_scalar(to[:, c, :], ident[:, :], newton[:, 1, c0 + c:c0 + c + 1], None, ALU.mult)
                ins.then_inc(diag_ready, 1)

            copied = [0]

            def take_spread(no, out):
                dve.wait_ge(spread_full, no + 1)
                dve.tensor_copy(out, ps[:, SPREAD_BANK, 0:HALF]).then_inc(rms_done, 1)
                copied[0] += 1
                dve.wait_ge(rms_done, copied[0])

            def pre_read(b, half):
                dve.wait_ge(pre_sums_full, 2 * b + half + 1)
                read_sums(ps[:, SUM_BANK, 0:TT], 0, TT, D_MODEL)
                dve.wait_ge(sums_read, norm(b, "pre", half) + 1)

            def pre_rms(b, half):
                inverse_root(TT)
                diagonals(diag, 0)
                take_spread(norm(b, "pre", half), r_pre[:, half, :])

            def post_rms(b, half):
                no = norm(b, "post", half)
                dve.wait_ge(sums_full, 2 * b + 4 * (b > 3) + half + 1)
                read_sums(ps[:, SPREAD_BANK, 0:TT], 0, TT, D_MODEL)
                dve.wait_ge(sums_read, no + 1)
                inverse_root(TT)
                diagonals(diag, 0)
                take_spread(no, r_post[:, half, :])

            def input_lo(b, half, k):
                dve.wait_ge(xg_hi, step(b, half, k) + 1)
                dve.scalar_tensor_tensor(xg[:, 1, k, cols(half)], x[:, k, cols(half)], v(f"pre{b}", k),
                                         xg[:, 0, k, cols(half)].bitcast(F32), ALU.mult, ALU.subtract
                                         ).then_inc(xg_done, 1)

            def apply(b, half, ks):
                if SUBLAYERS[b][0] == "ffn":
                    gamma, c = half_post, KT * b
                else:
                    gamma, c = vec, VEC["post0"] + KT * b
                pre = b + 1 < stages
                n = len(ks)
                for j in range(n + 2):
                    if j < n:
                        k = ks[j]
                        if step(b, half, k) >= 2:
                            dve.wait_ge(x_done, step(b, half, k) - 1)
                        dve.scalar_tensor_tensor(prod[:, k % 2, :], y[:, k, cols(half)],
                                                 gamma[:, c + k:c + k + 1], r_post[:, half, :],
                                                 ALU.mult, ALU.mult).then_inc(t_ready, 1)
                    if 1 <= j <= n:
                        k = ks[j - 1]
                        dve.wait_ge(t_ready, step(b, half, k) + 1)
                        dve.tensor_tensor(x[:, k, cols(half)], x[:, k, cols(half)], prod[:, k % 2, :],
                                          ALU.add).then_inc(x_done, 1)
                    if pre and j >= 2:
                        input_lo(b + 1, half, ks[j - 2])

            def scale_item(kind, q, bank, par, j, half):
                dve.wait_ge(up_full, q + 1)
                dst = y[:, 2 * j:2 * j + 2, cols(half)] if kind == "mla" else gu[:, par, :, :]
                dve.tensor_tensor(dst, ps[:, bank:bank + 2, 0:HALF],
                                  r_pre[:, half:half + 1, :].broadcast_to([P, 2, HALF]), ALU.mult
                                  ).then_inc(scaled, 1)

            def ffn_item(a, g, par, c, half):
                dve.wait_ge(act_done, a + 1)
                dve.tensor_tensor(prod[:, par, :], act_out[:, par, :], gu[:, par, 1, :], ALU.mult
                                  ).then_inc(prod_done, 1)
                dve.wait_ge(h_hi, g + 1)
                dve.tensor_tensor(h[:, 1, at(c), cols(half)], prod[:, par:par + 1, :],
                                  h[:, 0, at(c), cols(half)].bitcast(F32), ALU.subtract).then_inc(h_done, 1)

            def take_out(d, n, m, half, first, bias=None):
                dve.wait_ge(out_full, d + (n + 1))
                dst = y[:, at(m), cols(half)]
                src = ps[:, OUT_BANK + n % 2:OUT_BANK + n % 2 + 1, 0:HALF]
                if bias is not None:
                    dve.tensor_scalar(dst, src, bias, None, ALU.add).then_inc(y_done, 1)
                elif first:
                    dve.tensor_copy(dst, src).then_inc(y_done, 1)
                else:
                    dve.tensor_tensor(dst, dst, src, ALU.add).then_inc(y_done, 1)

            def sum_square(b, n, m, half):
                dve.wait_ge(sq_done, 2 * KT * b + n + 1)
                if m == 0:
                    ins = dve.tensor_copy(acc[:, half, :], sq[:, n % 2, :])
                else:
                    ins = dve.tensor_tensor(acc[:, half, :], acc[:, half, :], sq[:, n % 2, :], ALU.add)
                if m == KT - 1:
                    ins.then_inc(acc_done, 1)

            def finish(b, d, first, bias):
                for n, (m, half) in enumerate(LAST_OUTS):
                    if n == 13:
                        post_rms(b, 0)
                        if SUBLAYERS[b][0] == "mla":
                            dve.wait_ge(x_back, 16)
                    if n == 14:
                        apply(b, 0, range(KT // 2))
                    take_out(d, n, m, half, first, v(bias, m) if bias else None)
                    if n == 14:
                        apply(b, 0, range(KT // 2, KT))
                    sum_square(b, n, m, half)
                post_rms(b, 1)
                if b + 1 < stages:
                    pre_read(b + 1, 0)
                apply(b, 1, range(KT // 2))
                if b + 1 < stages:
                    kind, _, q, _ = SUBLAYERS[b + 1]
                    pre_rms(b + 1, 0)
                    scale_item(kind, q, START_BANKS[0], 0, 0, 0)
                apply(b, 1, range(KT // 2, KT))
                if b + 1 < stages:
                    scale_item(kind, q + 1, START_BANKS[1], 1, 1, 0)

            def glu(a, par, c, half, slot):
                dve.wait_ge(act_done, a + 1)
                spans = (((0, PROMPT, PAD), (PROMPT, HALF, SEG + PAD)) if half == 0
                         else ((0, HALF, SEG + PAD + HALF - PROMPT),))
                for f, t, to in spans:
                    dve.scalar_tensor_tensor(cin[:, slot, to:to + t - f], gu[:, par, 0, f:t], v("b_pw1", c),
                                             act_out[:, par, f:t], ALU.add, ALU.mult).then_inc(conv_in, 1)

            def depthwise(c, slot):
                if not isinstance(c, int) or c > 0:
                    dve.wait_ge(conv_done, c)
                for j in range(DVE_TAPS):
                    src, out = cin[:, slot, j:j + CONV_OUT], cacc[:, j % 2, :]
                    w = v("w_dw", c * TAPS + j)
                    if j >= 2:
                        dve.wait_ge(tap_done, c * DVE_TAPS + (j - 1))
                        ins = dve.scalar_tensor_tensor(out, src, w, out, ALU.mult, ALU.add)
                    elif j == 1:
                        ins = dve.tensor_scalar(out, src, w, None, ALU.mult)
                    else:
                        ins = dve.tensor_scalar(out, src, w, v("b_dw", c), ALU.mult, ALU.add)
                    ins.then_inc(tap_done, 1)
                dve.wait_ge(tap_done, c * DVE_TAPS + DVE_TAPS)
                dve.tensor_tensor(cacc[:, 0, :], cacc[:, 0, :], cacc[:, 1, :], ALU.add).then_inc(chains_done, 1)

            def convolved(c):
                dve.wait_ge(chains_done, c + 1)
                dve.wait_ge(taps_full, c + 1)
                dve.tensor_tensor(y[:, at(c), 0:PROMPT], cacc[:, 0:1, 0:PROMPT],
                                  ps[:, OUT_BANK:OUT_BANK + 1, 0:PROMPT], ALU.add)
                dve.tensor_tensor(y[:, at(c), PROMPT:TOK], cacc[:, 0:1, SEG:CONV_OUT],
                                  ps[:, OUT_BANK + 1:OUT_BANK + 2, 0:SAMPLE], ALU.add).then_inc(conv_done, 1)

            def layer_norm():
                dve.wait_ge(mean_full, 1)
                for n in range(2 * KT):
                    half, k = n // KT, n % KT
                    dve.tensor_tensor(y[:, k, cols(half)], y[:, k, cols(half)], ps[:, SPREAD_BANK + half, 0:HALF],
                                      ALU.subtract).then_inc(centred, 1)

                dve.wait_ge(dev_sq_used, 2 * KT)
                for half in range(2):
                    read_sums(ps[:, OUT_BANK + half, 0:TT], half * TT, TT, D_MODEL)
                dve.wait_ge(sums_read, norm(1, "inner", 1) + 1)
                inverse_root(2 * TT)
                for half in range(2):
                    diagonals(ln_diag[:, half, :, :], half * TT)

                def ln_lo(n):
                    half, k = n // KT, n % KT
                    dve.wait_ge(ln_hi, n + 1)
                    dve.tensor_tensor(xg[:, 1, k, cols(half)], act_out[:, k % 2, :],
                                      xg[:, 0, k, cols(half)].bitcast(F32), ALU.subtract).then_inc(ln_split, 1)

                for n in range(2 * KT):
                    half, k = n // KT, n % KT
                    if k == 0:
                        dve.wait_ge(spread_full, norm(1, "inner", half) + 1)
                    if n >= 2:
                        dve.wait_ge(ln_act, n - 1)
                    dve.scalar_tensor_tensor(prod[:, k % 2, :], y[:, k, cols(half)], v("ln_g", k),
                                             ps[:, SPREAD_BANK + half, 0:HALF], ALU.mult, ALU.mult).then_inc(ln_done, 1)
                    if n >= 1:
                        ln_lo(n - 1)
                ln_lo(2 * KT - 1)

            def rotate(src, half, n, put_lo):
                dve.wait_ge(swapped, n + 1)
                dve.tensor_tensor(rope_tmp[:, 1, :], src, table[:, 0, cols(half)], ALU.mult).then_inc(rope_part, 1)
                dve.tensor_tensor(rope_tmp[:, 2, :], rope_tmp[:, 0, :], table[:, 1, cols(half)], ALU.mult
                                  ).then_inc(rope_part, 1)
                dve.wait_ge(rope_part, n * 2 + 2)
                dve.tensor_tensor(rope_tmp[:, 3, :], rope_tmp[:, 1, :], rope_tmp[:, 2, :], ALU.add
                                  ).then_inc(rotated, 1)

            def attention(b, q):
                for n in range(4, 6):
                    scale_item("mla", q + n, STEADY_BANKS[n - 4], 0, 2, n - 4)
                dve.wait_ge(sums_full, 2 * b + 4)
                read_sums(ps[:, SUM_BANK, 0:2 * TT], 0, 2 * TT, Q_RANK)
                read_sums(ps[:, SUM_BANK, 2 * TT:4 * TT], 2 * TT, 2 * TT, KV_RANK)
                for g in range(2):
                    dve.tensor_copy(newton[:, 3, g:g + 1], ident[:, 0:1]).then_inc(sums_read, 1)
                dve.wait_ge(sums_read, norm(b, "inner") + 4)
                inverse_root(4 * TT)
                for g in range(4):
                    diagonals(lat_diag[:, g, :, :], g * TT)
                dve.wait_ge(spread_full, norm(b, "inner") + 4)

                def lat_lo(n):
                    dve.wait_ge(part_hi, n + 1)
                    dve.tensor_tensor(h[:, 1, n // 2, cols(n % 2)], prod[:, n % 2, :],
                                      h[:, 0, n // 2, cols(n % 2)].bitcast(F32), ALU.subtract
                                      ).then_inc(part_done, 1)

                for n in range(2 * LATENTS):
                    t, half = n // 2, n % 2
                    gamma = v("q_g", t) if t < QT else v("kv_g", t - QT)
                    if n >= 2:
                        dve.wait_ge(part_done, n - 1)
                    dve.scalar_tensor_tensor(prod[:, half, :], y[:, t, cols(half)], gamma,
                                             ps[:, LAT_BANKS[2 * (t >= QT) + half], 0:HALF], ALU.mult, ALU.mult
                                             ).then_inc(lat_f, 1)
                    if n >= 1:
                        lat_lo(n - 1)
                lat_lo(2 * LATENTS - 1)
                dve.wait_ge(table_loaded, 16)
                for half in range(2):
                    rotate(y[:, KR, cols(half)], half, half, None)
                    dve.wait_ge(part_hi, 2 * LATENTS + half + 1)
                    dve.tensor_tensor(h[:, 1, KR, cols(half)], rope_tmp[:, 3, :],
                                      h[:, 0, KR, cols(half)].bitcast(F32), ALU.subtract).then_inc(part_done, 1)
                dve.wait_ge(x_saved, 16)
                with dve.Fori(0, PAIRS) as p:
                    for n in range(PROJ):
                        bank, half = n % 4, n % 2
                        if n in (4, 5):
                            dve.wait_ge(proj_full, p * PROJ + (n + 1))
                            rotate(ps[:, bank, 0:HALF], half, p * 2 + (n - 2), None)
                        dve.wait_ge(part_hi, p * PROJ + (LAT_PARTS + n + 1))
                        src = ps[:, bank, 0:HALF]
                        if n < 4:
                            hi, lo = (qn_r[:, i, n // 2, cols(half)] for i in range(2))
                        elif n < 6:
                            hi, lo = (qr_r[:, i, cols(half)] for i in range(2))
                            src = rope_tmp[:, 3, :]
                        elif n < 10:
                            hi, lo = (kn_r[:, i, (n - 6) // 2, cols(half)] for i in range(2))
                        else:
                            t = (n - 10) * 2
                            hi, lo = (v_r[:, i, t:t + 2, :] for i in range(2))
                            src = ps[:, bank, :].rearrange("p (a n) -> p a n", a=2)
                        dve.tensor_tensor(lo, src, hi.bitcast(F32), ALU.subtract).then_inc(part_done, 1)

                    def row_max(i):
                        nk, s = Q_TILES[i][2][1], i % SCORE_BUFS
                        dve.wait_ge(s_full, p * 12 + (i + 1))
                        dve.tensor_reduce(soft[:, 0, s:s + 1], ps[:, SCORE_BANKS[s], 0:nk], AX_X, ALU.max).then_inc(s_max, 1)
                        dve.wait_ge(s_max, p * 12 + (i + 1))
                        dve.tensor_scalar(soft[:, 1, s:s + 1], soft[:, 0, s:s + 1], -SCALE, None, ALU.mult
                                          ).then_inc(s_nmax, 1)

                    def divide(i):
                        nk, s = Q_TILES[i][2][1], i % SCORE_BUFS
                        dve.wait_ge(s_exp, p * 12 + (i + 1))
                        dve.reciprocal(soft[:, 3, s:s + 1], soft[:, 2, s:s + 1]).then_inc(s_inv, 1)
                        dve.wait_ge(s_inv, p * 12 + (i + 1))
                        dve.tensor_scalar(probs[:, s, 0:nk], probs[:, s, 0:nk], soft[:, 3, s:s + 1], None,
                                          ALU.mult).then_inc(p_done, 1)

                    def turned(j):
                        nk = Q_TILES[2 * j][2][1]
                        dve.wait_ge(pt_hi, p * 6 + (j + 1))
                        for g in range(nk // 256):
                            ins = dve.tensor_tensor(pt[j % 2][1][:, 2 * g:2 * g + 2, :],
                                                    ps[:, 6 + g, :].rearrange("p (a n) -> p a n", a=2),
                                                    pt[j % 2][0][:, 2 * g:2 * g + 2, :].bitcast(F32),
                                                    ALU.subtract)
                        ins.then_inc(pt_done, 1)

                    def output(j):
                        head, q0, _ = Q_TILES[2 * j]
                        dve.wait_ge(o_hi, p * 6 + (j + 1))
                        dve.tensor_tensor(xg[:, 1, at(p * 2 + head), q0:q0 + 256], ps[:, j % 2:j % 2 + 1, 0:256],
                                          xg[:, 0, at(p * 2 + head), q0:q0 + 256].bitcast(F32), ALU.subtract
                                          ).then_inc(o_done, 1)

                    for i in range(18):
                        if i < 12:
                            row_max(i)
                        if 1 <= i < 13:
                            divide(i - 1)
                        if i >= 4 and i % 2 == 0 and i < 16:
                            turned((i - 4) // 2)
                        if i >= 7 and i % 2 == 1:
                            output((i - 7) // 2)

            dve.wait_ge(vec_loaded, 16)
            dve.tensor_scalar(half_post[:, :], vec[:, VEC["post0"]:VEC["post0"] + 6 * KT], 0.5, None,
                              ALU.mult).then_inc(consts, 1)
            dve.wait_ge(ident_loaded, 16)
            for i in range(CREDIT):
                dve.memset(acc[:, i, :], 0.0).then_inc(y_done, 1)
            for k in range(KT):
                input_lo(0, 0, k)
            pre_read(0, 0)
            for k in range(KT // 2):
                input_lo(0, 1, k)
            pre_rms(0, 0)
            scale_item("ffn", 0, START_BANKS[0], 0, 0, 0)
            for k in range(KT // 2, KT):
                input_lo(0, 1, k)
            scale_item("ffn", 1, START_BANKS[1], 1, 1, 0)
            dve.wait_ge(consts, 1)
            for b, (kind, unit, q, d) in enumerate(todo):
                g, a = ffn_items(b), act_items(b)
                if kind == "ffn":
                    for n, (c0, nc_) in enumerate(BLOCKS):
                        qb, gb, ab, db = q + 2 * c0, g + 2 * c0, a + 2 * c0, d + 2 * KT * n
                        if n == 0:
                            for m, (j, half) in enumerate(STARTING):
                                if m == 2:
                                    pre_read(b, 1)
                                    pre_rms(b, 1)
                                if m >= 2:
                                    scale_item(kind, qb + m, START_BANKS[m], m % 2, j, half)
                                ffn_item(ab + m, gb + m, m % 2, j, half)
                        with dve.Fori(1 if n == 0 else 0, nc_ // 2) as i:
                            for m, (j, half) in enumerate(STEADY):
                                scale_item(kind, i * 4 + (qb + m), STEADY_BANKS[m], m % 2, j, half)
                                ffn_item(i * 4 + (ab + m), i * 4 + (gb + m), m % 2, i * 2 + j, half)
                        if n < len(BLOCKS) - 1:
                            with dve.Fori(0, KT // 4) as i:
                                for m in range(8):
                                    take_out(i * 8 + db, m, i * 4 + m // 2, m % 2, n == 0)
                    finish(b, d + 2 * KT * (len(BLOCKS) - 1), False, None)
                elif kind == "conv":
                    dve.memset(cin[:, :, :], 0.0).then_inc(pads, 1)
                    dve.wait_ge(pads, 1)
                    for m, (j, half) in enumerate(STARTING):
                        if m == 2:
                            pre_read(b, 1)
                            pre_rms(b, 1)
                        if m >= 2:
                            scale_item(kind, q + m, START_BANKS[m], m % 2, j, half)
                        glu(a + m, m % 2, j, half, j)
                    dve.wait_ge(conv_in, 6)
                    depthwise(0, 0)
                    convolved(0)
                    depthwise(1, 1)
                    with dve.Fori(1, KT // 2) as i:
                        for m, (j, half) in enumerate(STEADY):
                            scale_item(kind, i * 4 + (q + m), STEADY_BANKS[m], m % 2, j, half)
                            glu(i * 4 + (a + m), m % 2, i * 2 + j, half, j)
                            if half == 1:
                                convolved(i * 2 + (j - 1))
                                dve.wait_ge(conv_in, i * 6 + (3 * j + 3))
                                depthwise(i * 2 + j, j)
                    convolved(KT - 1)
                    layer_norm()
                    finish(b, d, False, "b_pw2")
                else:
                    for m in range(2, 4):
                        if m == 2:
                            pre_read(b, 1)
                            pre_rms(b, 1)
                        scale_item(kind, q + m, START_BANKS[m], 0, STARTING[m][0], 1)
                    attention(b, q)
                    finish(b, d, True, None)


WEIGHT_SETS = (("ffn", "l0_ffn1_"), ("conv", "l0_conv_"), ("ffn", "l0_ffn2_"),
               ("ffn", "l1_ffn1_"), ("mla", "l1_mla_"), ("ffn", "l1_ffn2_"))
PRE = ("l0_ffn1_pre_g", "l0_mix_pre_g", "l0_ffn2_pre_g", "l1_ffn1_pre_g", "l1_mix_pre_g", "l1_ffn2_pre_g")
POST = tuple(n.replace("_pre_", "_post_") for n in PRE)


def kernel(**inputs):
    import numpy as np
    import concourse.bacc as bacc
    from concourse.bass_utils import run_bass_kernel_spmd

    a = {k: np.asarray(t) for k, t in inputs.items()}

    def tiles(w, m):
        return w[:, m * P:(m + 1) * P].reshape(-1, P, P).transpose(1, 0, 2)

    units = np.zeros((UNITS, P, KT, P), np.float32)
    u = 0

    def put(t):
        nonlocal u
        units[u, :, :t.shape[1]] = t
        u += 1

    for kind, pre in WEIGHT_SETS:
        if kind == "ffn":
            gate, up, down = (a[pre + n] for n in ("w_gate", "w_up", "w_down"))
            for c0, nc_ in BLOCKS:
                for c in range(c0, c0 + nc_):
                    put(tiles(gate, c))
                    put(tiles(up, c))
                for m in range(KT):
                    put(tiles(down, m)[:, c0:c0 + nc_])
        elif kind == "conv":
            for c in range(KT):
                put(tiles(a[pre + "w_pw1"], c))
                put(tiles(a[pre + "w_pw1"], KT + c))
            for m in range(KT):
                put(tiles(a[pre + "w_pw2"], m))
        else:
            dq, dkv, uq = a[pre + "w_dq"], a[pre + "w_dkv"], a[pre + "w_uq"]
            for m in range(QT):
                put(tiles(dq, m))
            for m in range(KVT):
                put(tiles(dkv, m))
            key = dkv[:, KV_RANK:]
            put(tiles(np.concatenate([key, key], 1), 0))
            uq = uq.reshape(Q_RANK, HEADS, NOPE + ROPE)
            for p in range(PAIRS):
                heads = (2 * p, 2 * p + 1)
                put(np.concatenate([tiles(uq[:, i, :NOPE], 0) for i in heads], 1))
                put(tiles(np.concatenate([uq[:, i, NOPE:] for i in heads], 1), 0))
                put(np.concatenate([tiles(a[pre + "w_uk"], i) for i in heads], 1))
                uv = a[pre + "w_uv"][:, heads[0] * VDIM:(heads[1] + 1) * VDIM]
                put(uv.reshape(KVT, P, 2, P).transpose(1, 0, 2, 3).reshape(P, 2 * KVT, P))
            for m in range(KT):
                put(tiles(a[pre + "w_o"], m))
    assert u == UNITS

    vectors = np.zeros((P, VECS), np.float32)

    def column(name, t):
        t = t.reshape(-1, P).T
        vectors[:, VEC[name]:VEC[name] + t.shape[1]] = t

    for i in range(6):
        column(f"pre{i}", a[PRE[i]])
        column(f"post{i}", a[POST[i]])
    for name in ("b_pw1", "b_dw", "ln_g", "ln_b", "b_pw2"):
        column(name, a["l0_conv_" + name])
    column("w_dw", a["l0_conv_w_dw"].reshape(TAPS, KT, P).transpose(1, 0, 2))
    column("q_g", a["l1_mla_q_norm_g"])
    column("kv_g", a["l1_mla_kv_norm_g"])

    freq = (10000.0 ** (-np.arange(0, ROPE, 2) / ROPE)).astype(np.float32)
    place = np.concatenate([np.arange(PROMPT), np.arange(SAMPLE)]).astype(np.float32)
    angle = freq[:, None] * place[None, :]
    cos, sin = np.cos(angle), np.sin(angle)
    rope = np.stack([np.concatenate([cos, cos] * 2), np.concatenate([-sin, sin] * 2)], 1)

    x = np.concatenate([a["x_prompt"][0], a["x_sample"][0]])
    arrays = {"x_in": np.ascontiguousarray(x.T.reshape(KT, P, TOK).transpose(1, 0, 2)),
              "weights": units.reshape(UNITS, P, UNIT), "vectors": vectors,
              "rope_in": np.ascontiguousarray(rope.astype(np.float32)), "ident_in": np.eye(P, dtype=np.float32)}

    nc = bacc.Bacc("TRN2", target_bir_lowering=False, num_devices=1, dynamic_dma_scratch_size=1024)
    args = [nc.dram_tensor(n, t.shape, F32, kind="ExternalInput").ap() for n, t in arrays.items()]
    out = nc.dram_tensor("y_out", (P, KT, TOK), F32, kind="ExternalOutput").ap()
    trunk(nc, *args, out)
    got = run_bass_kernel_spmd(nc, [arrays], core_ids=[0]).results[0]["y_out"]
    y = np.asarray(got).transpose(1, 0, 2).reshape(D_MODEL, TOK).T
    return np.ascontiguousarray(y[:PROMPT])[None], np.ascontiguousarray(y[PROMPT:])[None]
```

```python
from contextlib import ExitStack

import concourse.bass as bass
from concourse import mybir

F32 = mybir.dt.float32
F32R = mybir.dt.float32r
I32 = mybir.dt.int32
ALU = mybir.AluOpType
ACT = mybir.ActivationFunctionType
AX_X = mybir.AxisListType.X

P = 128
D_MODEL = 1024
KT = D_MODEL // P
D_FF = 2816
PROMPT, SAMPLE = 256, 512
TOK = PROMPT + SAMPLE
HALF = TOK // 2
TT = HALF // P
EPS = 1e-6

CHUNKS = D_FF // P
BLOCKS = ((0, 6), (6, 8), (14, 8))
RING = 4
UNIT = KT * P

TAPS = 31
PE_TAPS = 9
DVE_TAPS = TAPS - PE_TAPS
PAD = TAPS // 2
SEG = PROMPT + 2 * PAD
PADDED = SEG + SAMPLE + 2 * PAD
CONV_OUT = PADDED - 2 * PAD

HEADS = 8
NOPE, ROPE, VDIM = 128, 64, 128
Q_RANK, KV_RANK = 384, 256
QT, KVT = Q_RANK // P, KV_RANK // P
PAIRS = HEADS // 2
SCALE = float(NOPE + ROPE) ** -0.5

FFN_UNITS = 2 * CHUNKS + KT * len(BLOCKS)
SUBLAYERS = []
_unit = _up = _out = 0
for _kind in ("ffn", "conv", "ffn", "ffn", "mla", "ffn"):
    _n = {"ffn": (FFN_UNITS, 2 * CHUNKS, 2 * KT * len(BLOCKS)),
          "conv": (3 * KT, 2 * KT, 2 * KT),
          "mla": (2 * QT + 4 * PAIRS + KT, 2 * QT, 2 * KT)}[_kind]
    SUBLAYERS.append((_kind, _unit, _up, _out))
    _unit, _up, _out = _unit + _n[0], _up + _n[1], _out + _n[2]
UNITS = _unit

VEC = {}
_col = 0
for _name, _n in ([(f"pre{i}", KT) for i in range(6)] + [(f"post{i}", KT) for i in range(6)]
                  + [("b_pw1", 2 * KT), ("b_dw", KT), ("ln_g", KT), ("ln_b", KT), ("b_pw2", KT),
                     ("w_dw", KT * TAPS), ("q_g", QT), ("kv_g", KVT)]):
    VEC[_name] = _col
    _col += _n
VECS = _col


CREDIT = 2
ROOT_STEPS = 11
SCORE_BUFS = 3


def at(start, count=1):
    return bass.ds(start, count)


def trunk(nc, x_in, weights, vectors, rope_in, ident_in, y_out, stages=len(SUBLAYERS)):
    with ExitStack() as ctx:
        place, spot = [(nc.sbuf_base + 31) // 32 * 32], {}

        def sbuf(name, shape, dt=F32):
            size = 4
            for n in shape[1:]:
                size *= n
            spot[name] = place[0]
            place[0] += (size + 31) // 32 * 32
            return nc.alloc_sbuf_tensor_at(name, shape, dt, offset=spot[name])

        def over(name, shape, offset, dt=F32):
            return nc.alloc_sbuf_tensor_at(name, shape, dt, offset=offset)

        def sem(name):
            return ctx.enter_context(nc.semaphore(name))

        x = sbuf("x", [P, KT, TOK])
        xg = sbuf("xg", [P, 2, KT, TOK], F32R)
        h = sbuf("h", [P, 2, KT, TOK], F32R)
        y = sbuf("y", [P, KT, TOK])
        w_ring = sbuf("w_ring", [P, RING, 2, UNIT], F32R)
        w_stage = sbuf("w_stage", [P, RING, UNIT])
        vec = sbuf("vec", [P, VECS])
        half_post = sbuf("half_post", [P, 6 * KT])
        gu = sbuf("gu", [P, 2, 2, HALF])
        act_out = sbuf("act_out", [P, 2, HALF])
        prod = sbuf("prod", [P, 2, HALF])
        sq = sbuf("sq", [P, 2, HALF])
        acc = sbuf("acc", [P, 2, HALF])
        pre_acc = sbuf("pre_acc", [P, HALF])
        r_post = sbuf("r_post", [P, 2, HALF])
        r_pre = sbuf("r_pre", [P, 2, HALF])
        mean_w = sbuf("mean_w", [P, P])
        ones_w = sbuf("ones_w", [P, P])
        ident = sbuf("ident", [P, P])
        diag = sbuf("diag", [P, TT, P])
        newton = sbuf("newton", [P, 4, 4 * TT])
        soft = sbuf("soft", [P, 4, SCORE_BUFS])
        carrier = sbuf("carrier", [P, 4])
        zero = sbuf("zero", [P, 1])
        assert place[0] <= nc.sbuf_usable_end, place[0] - nc.sbuf_usable_end

        cin = over("cin", [P, 2, PADDED], spot["h"])
        cacc = over("cacc", [P, 2, CONV_OUT], spot["h"] + 2 * PADDED * 4)
        ln_diag = over("ln_diag", [P, 2, TT, P], spot["h"])
        tap_w = over("tap_w", [P, 2, PE_TAPS, P], spot["h"] + (2 * PADDED + 2 * CONV_OUT + 7) * 4 // 32 * 32)
        KV0, KR = QT, QT + KVT
        v_r = over("v_r", [P, 2, TOK // P, 2 * VDIM], spot["y"], F32R)
        qn_r = over("qn_r", [P, 2, 2, TOK], spot["y"] + TOK // P * 2 * VDIM * 8, F32R)
        kn_r = over("kn_r", [P, 2, 2, TOK], spot["x"], F32R)
        KEYS = SAMPLE // P
        pt_a = [over(f"pt_a{i}", [P, KEYS, 256], spot["x"] + 2 * TOK * 8 + i * KEYS * 1024, F32R) for i in range(2)]
        pt_b = [over(f"pt_b{i}", [P, KEYS, 256], spot["h"] + (i * KT + 6) * TOK * 4, F32R) for i in range(2)]
        pt = [pt_a, pt_b]
        qr_r = over("qr_r", [P, 2, TOK], spot["sq"], F32R)
        rope_tmp = over("rope_tmp", [P, 4, HALF], spot["act_out"])
        table = over("table", [P, 2, TOK], spot["r_post"])
        probs = over("probs", [P, SCORE_BUFS, SAMPLE], spot["gu"])
        lat_diag = over("lat_diag", [P, 4, TT, P], spot["act_out"])

        ps = ctx.enter_context(nc.psum_tensor("ps", [P, 8, 512], F32))
        OUT_BANK, SPREAD_BANK, SUM_BANK = 4, 6, 7
        SCORE_BANKS = (4, 5, 3)
        LAT_BANKS = (0, 1, 6, 7)
        x_kept = nc.dram_tensor("x_kept", (P, KT, TOK), F32, kind="Internal").ap()

        x_loaded = [sem(f"x_loaded{half}") for half in range(2)]
        vec_loaded, ident_loaded = sem("vec_loaded"), sem("ident_loaded")
        w_loaded = [sem(f"w_loaded{s}") for s in range(RING)]
        mean_ready, consts = sem("mean_ready"), sem("consts")
        w_hi, w_split, w_used = sem("w_hi"), sem("w_split"), sem("w_used")
        up_full, scaled, act_done, prod_done = sem("up_full"), sem("scaled"), sem("act_done"), sem("prod_done")
        h_hi, h_done = sem("h_hi"), sem("h_done")
        out_full, y_done, sq_done, acc_done = sem("out_full"), sem("y_done"), sem("sq_done"), sem("acc_done")
        sums_full, sums_read, newton_step = sem("sums_full"), sem("sums_read"), sem("newton_step")
        diag_ready, spread_full, rms_done = sem("diag_ready"), sem("spread_full"), sem("rms_done")
        t_ready, x_done, xg_hi, xg_done = sem("t_ready"), sem("x_done"), sem("xg_hi"), sem("xg_done")
        pre_sq, pre_sq_used, pre_sums_full = sem("pre_sq"), sem("pre_sq_used"), sem("pre_sums_full")
        pads, conv_in, tap_done, conv_done = sem("pads"), sem("conv_in"), sem("tap_done"), sem("conv_done")
        tap_w_ready, taps_full, chains_done = sem("tap_w_ready"), sem("taps_full"), sem("chains_done")
        mean_full, centred, dev_sq = sem("mean_full"), sem("centred"), sem("dev_sq")
        dev_sq_used = sem("dev_sq_used")
        ln_done, ln_act, ln_hi, ln_split = sem("ln_done"), sem("ln_act"), sem("ln_hi"), sem("ln_split")
        x_saved, x_back, table_loaded = sem("x_saved"), sem("x_back"), sem("table_loaded")
        lat_sq, lat_f = sem("lat_sq"), sem("lat_f")
        proj_full, part_hi, part_done = sem("proj_full"), sem("part_hi"), sem("part_done")
        swapped, rope_part, rotated = sem("swapped"), sem("rope_part"), sem("rotated")
        s_full, s_max, s_nmax, s_exp, s_inv, p_done = (
            sem(n) for n in ("s_full", "s_max", "s_nmax", "s_exp", "s_inv", "p_done"))
        tr_full, pt_hi, pt_done = sem("tr_full"), sem("pt_hi"), sem("pt_done")
        pv_full, o_hi, o_done = sem("pv_full"), sem("o_hi"), sem("o_done")
        stored = sem("stored")

        todo = SUBLAYERS[:stages]
        units = SUBLAYERS[stages][1] if stages < len(SUBLAYERS) else UNITS

        def cols(half):
            return slice(half * HALF, (half + 1) * HALF)

        def v(name, k):
            return vec[:, at(VEC[name] + k)]

        def step(b, half, k):
            return (b * 2 + half) * KT + k

        def ffn_items(b):
            return 2 * CHUNKS * sum(kind == "ffn" for kind, *_ in SUBLAYERS[:b])

        def act_items(b):
            return ffn_items(b) + 2 * KT * (b > 1)

        def norm(b, what, half=0):
            base = 4 * b + 2 * (b > 1) + 4 * (b > 4)
            return base + half + {"pre": 0, "inner": 2, "post": 2 + 2 * (b == 1) + 4 * (b == 4)}[what]

        STARTING = ((0, 0), (1, 0), (0, 1), (1, 1))
        STEADY = ((0, 0), (0, 1), (1, 0), (1, 1))
        START_BANKS = (0, 2, OUT_BANK, 2)
        STEADY_BANKS = (0, 2, 0, 2)
        OUTS = tuple((m, half) for m in range(KT) for half in range(2))
        LAST_OUTS = OUTS[:8] + tuple((m, half) for half in range(2) for m in range(KT // 2, KT))

        def square_place(half, k):
            if half == 0 and k < 4:
                return gu[:, k // 2, k % 2, :]
            if half == 0 and k < 6:
                return act_out[:, k - 4, :]
            return sq[:, k % 2, :]

        DEV_SQ = [gu[:, 0, 0, :], gu[:, 0, 1, :], gu[:, 1, 0, :], gu[:, 1, 1, :], sq[:, 0, :], sq[:, 1, :]]
        Q_TILES = [(i // 6, (i % 6) * P, (0, PROMPT) if i % 6 < 2 else (PROMPT, SAMPLE)) for i in range(12)]
        LAT_SQ = [gu[:, 0, 0, :], gu[:, 0, 1, :], gu[:, 1, 0, :], gu[:, 1, 1, :], act_out[:, 0, :],
                  act_out[:, 1, :], prod[:, 0, :], prod[:, 1, :], sq[:, 0, :], sq[:, 1, :]]
        LATENTS = QT + KVT
        LAT_PARTS = 2 * (LATENTS + 1)
        PROJ = 13
        PROJ_BANKS = (2, 3, 4, 5, 6, 7, 2, 3, 0, 1, 2, 0, 1)
        QUERY, KEY, VAL = 2, 6, 10
        EARLY = 4
        PARTS = (0, 2, 1, 3, 4, 5, 6, 7, 8, 9, 10, 11, 12)
        GROUPS = [sum(Q_TILES[2 * i][2][1] // 256 for i in range(j)) for j in range(7)]

        block = ctx.enter_context(nc.Block())

        @block.sync
        def _(sp):
            sp.dma_start(vec[:, :], vectors).then_inc(vec_loaded, 16)
            for s in range(RING):
                sp.dma_start(w_stage[:, s, :], weights[s]).then_inc(w_loaded[s], 16)
                if s == 1:
                    sp.dma_start(x[:, :, cols(1)], x_in[:, :, cols(1)]).then_inc(x_loaded[1], 16)
            sp.dma_start(ident[:, :], ident_in).then_inc(ident_loaded, 16)

            def load(u, s):
                sp.wait_ge(w_split, u - (RING - 1))
                sp.dma_start(w_stage[:, at(s), :], weights[at(u), :, :].rearrange("a p n -> p a n")
                             ).then_inc(w_loaded[s], 16)

            full = units // RING
            with sp.Fori(1, full) as i:
                for s in range(RING):
                    load(i * RING + s, s)
            for u in range(full * RING, units):
                load(u, u % RING)
            for half in range(2):
                sp.wait_ge(x_done, step(stages - 1, half, KT - 1) + 1)
                sp.dma_start(y_out[:, :, cols(half)], x[:, :, cols(half)]).then_inc(stored, 16)
            sp.wait_ge(stored, 32)

        @block.gpsimd
        def _(pool):
            pool.memset(ones_w[:, :], 1.0).then_inc(mean_ready, 1)
            pool.memset(zero[:, :], 0.0).then_inc(mean_ready, 1)
            pool.memset(mean_w[:, :], 1.0 / D_MODEL).then_inc(mean_ready, 1)
            pool.wait_ge(mean_ready, 2)

            def split(u, s, loads):
                pool.wait_ge(w_loaded[s], 16 * loads)
                if not isinstance(u, int) or u >= RING:
                    pool.wait_ge(w_used, u - (RING - 1))
                pool.tensor_tensor(w_ring[:, s, 0, :], w_stage[:, s, :], zero[:, 0:1].broadcast_to([P, UNIT]),
                                   ALU.add).then_inc(w_hi, 1)
                pool.wait_ge(w_hi, u + 1)
                pool.tensor_tensor(w_ring[:, s, 1, :], w_stage[:, s, :], w_ring[:, s, 0, :].bitcast(F32),
                                   ALU.subtract).then_inc(w_split, 1)

            def sum_squares(b, half):
                for k in range(1, KT):
                    pool.wait_ge(pre_sq, step(b, half, k) + 1)
                    one = square_place(half, 0) if k == 1 else pre_acc[:, :]
                    if k == 1 and b + half > 0:
                        pool.wait_ge(pre_sums_full, 2 * b + half)
                    if k > 1:
                        pool.wait_ge(pre_sq_used, step(b, half, k))
                    pool.tensor_tensor(pre_acc[:, :], one, square_place(half, k), ALU.add
                                       ).then_inc(pre_sq_used, 2 if k == 1 else 1)

            for s in range(RING):
                split(s, s, 1)
            for b, (_, unit, _, _) in enumerate(todo):
                for half in range(2):
                    sum_squares(b, half)
                lo = unit + RING
                hi = min(SUBLAYERS[b + 1][1] + RING if b + 1 < len(SUBLAYERS) else units, units)
                with pool.Fori(0, (hi - lo) // RING) as i:
                    for s in range(RING):
                        split(i * RING + (lo + s), (lo + s) % RING, i + ((lo + s) // RING + 1))
                for u in range(lo + (hi - lo) // RING * RING, hi):
                    split(u, u % RING, u // RING + 1)

        @block.tensor
        def _(pe):
            def mm3(out, w, v, start, stop, release=False):
                mm = pe.matmul(out, w[0], v[0], start=start, stop=False)
                if release:
                    mm.then_inc(w_used, 1)
                pe.matmul(out, w[1], v[0], start=False, stop=False)
                return pe.matmul(out, w[0], v[1], start=False, stop=stop)

            def tile(s, t, n=P):
                return [w_ring[:, s % RING, i, t * P:t * P + n] for i in range(2)]

            def both(t, k, c):
                return [t[:, i, k, c] for i in range(2)]

            def sums(bank, c0, squares, first, last):
                for c in range(TT):
                    mm = pe.matmul(ps[:, bank, c0 + c:c0 + c + 1], squares[:, c * P:(c + 1) * P], ones_w[:, 0:1],
                                   start=first and c == 0, stop=last, skip_group_check=True)
                return mm

            def spread(no, bank=SPREAD_BANK, d=None):
                pe.wait_ge(diag_ready, no + 1)
                pe.matmul(ps[:, bank, 0:HALF], ones_w[:, :], (diag[:, :, :] if d is None else d
                          ).rearrange("p a n -> p (a n)"), start=True, stop=True).then_inc(spread_full, 1)

            def pre_square(b, half):
                pe.wait_ge(pre_sq_used, step(b, half, KT - 1) + 1)
                if half == 1:
                    pe.wait_ge(sums_read, norm(b, "pre") + 1)
                sums(SUM_BANK, 0, pre_acc[:, :], True, True).then_inc(pre_sums_full, 1)

            def post_square(b, half):
                pe.wait_ge(acc_done, 2 * b + half + 1)
                sums(SPREAD_BANK, 0, acc[:, half, :], True, True).then_inc(sums_full, 1)

            def up_item(q, bank, s, half, release, starting=None, n=None):
                for k in range(KT):
                    if starting is not None and n == 3 and k == KT - 3:
                        pre_square(starting, 1)
                    if starting is not None and n in (0, 2):
                        pe.wait_ge(xg_done, step(starting, half, k) + 1)
                    for g in range(2):
                        mm = mm3(ps[:, bank + g, 0:HALF], tile(s + g, k), both(xg, k, cols(half)),
                                 k == 0, k == KT - 1, release=release and k == 0 and g == 0)
                        if half == 1 and k == KT - 1 and g == 0:
                            mm.then_inc(w_used, 1)
                    if starting is not None and starting > 0 and (n, k) == (0, KT - 1):
                        post_square(starting - 1, 1)
                    if starting is not None and starting > 0 and (n, k) == (1, KT // 2 - 1):
                        spread(norm(starting - 1, "post", 1))
                    if starting is not None and (n, k) == (1, KT - 3):
                        pre_square(starting, 0)
                mm.then_inc(up_full, 1)
                if starting is not None and n >= 2:
                    spread(norm(starting, "pre", n - 2))

            def up_start(b, unit, q):
                for n, (j, half) in enumerate(STARTING):
                    pe.wait_ge(w_split, unit + 2 * j + 2)
                    if n == 2:
                        pe.wait_ge(y_done, SUBLAYERS[b][3] + CREDIT)
                    elif q + n >= 2:
                        pe.wait_ge(scaled, q + n - 1)
                    up_item(q + n, START_BANKS[n], unit + 2 * j, half, n == 3 or (n == 0 and b > 0),
                            starting=b, n=n)

            def up_pair(q, unit, s, items=(0, 1, 2, 3)):
                for n in items:
                    j, half = STEADY[n]
                    if half == 0:
                        pe.wait_ge(w_split, unit + (2 * j + 2))
                    pe.wait_ge(scaled, q + (n - 1))
                    up_item(q, STEADY_BANKS[n], s + 2 * j, half, half == 0)

            def out_items(d, unit, s, src, nk, outs, release_first=True, need=None, each=None,
                          last_of=None):
                m0 = outs[0][0]
                for n, (m, half) in enumerate(outs):
                    pe.wait_ge(w_split, unit + (m - m0 + 1))
                    pe.wait_ge(y_done, d + (n - 1 + CREDIT))
                    if need is not None and n < 2:
                        pe.wait_ge(*need[n])
                    release = (n > 0 and outs[n - 1][1] == 1) or (n == 0 and release_first)
                    for k in range(nk):
                        if each is not None and n < 2:
                            pe.wait_ge(each, n * nk + k + 1)
                        mm = mm3(ps[:, OUT_BANK + n % 2, 0:HALF], tile(s + m - m0, k), both(src, k, cols(half)),
                                 k == 0, k == nk - 1, release=release and k == 0)
                        if last_of is not None and (n, k) == (12, nk // 2):
                            post_square(last_of, 0)
                        if last_of is not None and (n, k) == (13, nk // 2 - 1):
                            spread(norm(last_of, "post", 0))
                    mm.then_inc(out_full, 1)

            def conv_taps(c, slot):
                pe.wait_ge(conv_in, 5 if isinstance(c, int) and c == 0 else c * 3 + 3)
                pe.wait_ge(tap_w_ready, c + 1)
                if not isinstance(c, int) or c > 0:
                    pe.wait_ge(conv_done, c)
                for i in range(PE_TAPS):
                    for bank, t, n in ((OUT_BANK, 0, PROMPT), (OUT_BANK + 1, SEG, SAMPLE)):
                        mm = pe.matmul(ps[:, bank, 0:n], tap_w[:, slot, i, :],
                                       cin[:, slot, t + DVE_TAPS + i:t + DVE_TAPS + i + n],
                                       start=i == 0, stop=i == PE_TAPS - 1)
                mm.then_inc(taps_full, 1)

            def mean(c, last=False):
                pe.wait_ge(conv_done, c + 1)
                for half in range(2):
                    mm = pe.matmul(ps[:, SPREAD_BANK + half:SPREAD_BANK + half + 1, 0:HALF], mean_w[:, :],
                                   y[:, at(c), cols(half)], start=False, stop=last)
                return mm

            def attention(b, unit):
                pe.wait_ge(ident_loaded, 16)
                up_q = SUBLAYERS[b][2] + 4
                for n in range(2):
                    pe.wait_ge(w_split, unit + 6)
                    pe.wait_ge(scaled, up_q + n - 1)
                    up_item(up_q + n, STEADY_BANKS[n], unit + 4, n, n == 0)
                pe.wait_ge(lat_sq, 2 * LATENTS)
                for g in range(4):
                    tiles = range(QT) if g < 2 else range(QT, LATENTS)
                    for t in tiles:
                        mm = sums(SUM_BANK, g * TT, LAT_SQ[2 * t + g % 2], t == tiles[0], t == tiles[-1])
                        if g == 0 and t == 0:
                            mm.then_inc(w_used, 1)
                    mm.then_inc(sums_full, 1)
                for g in range(4):
                    spread(norm(b, "inner") + g, LAT_BANKS[g], lat_diag[:, g, :, :])

                base = unit + 2 * QT
                s = base % RING

                def project_queries(p, ns):
                    for n in ns:
                        for k in range(QT):
                            w = tile(s, k) if n < QUERY else tile(s + 1, (n - QUERY) // 2 * QT + k)
                            mm = mm3(ps[:, PROJ_BANKS[n], 0:HALF], w, both(h, k, cols(n % 2)),
                                     k == 0, k == QT - 1, release=n == QUERY and k == 0)
                        mm.then_inc(proj_full, 1)

                def early(p):
                    pe.wait_ge(w_split, p * 4 + (base + 2))
                    project_queries(p, range(EARLY))

                def others(p):
                    pe.wait_ge(part_done, 2 * LATENTS)
                    pe.wait_ge(pt_done, p * GROUPS[-1])
                    project_queries(p, range(EARLY, KEY))
                    for n in range(KEY, PROJ):
                        if n in (KEY, VAL):
                            pe.wait_ge(w_split, p * 4 + (base + (KEY, VAL).index(n) + 3))
                        if n in (KEY + 2, KEY + 3):
                            pe.wait_ge(o_done, p * 6)
                        else:
                            before = max(i for i in range(n) if PROJ_BANKS[i] == PROJ_BANKS[n])
                            pe.wait_ge(part_done, p * PROJ + (LAT_PARTS + PARTS.index(before) + 1))
                        bank, rel = PROJ_BANKS[n], n in (KEY, VAL)
                        if n < VAL:
                            for k in range(KVT):
                                mm = mm3(ps[:, bank, 0:HALF], tile(s + 2, (n - KEY) // 2 * KVT + k),
                                         both(h, KV0 + k, cols(n % 2)), k == 0, k == KVT - 1,
                                         release=rel and k == 0)
                        else:
                            for i in range(2):
                                t = (n - VAL) * 2 + i
                                for k in range(KVT):
                                    mm = mm3(ps[:, bank, i * 256:(i + 1) * 256],
                                             both(h, KV0 + k, slice(t * P, (t + 1) * P)),
                                             tile(s + 3, 2 * k, 256), k == 0, k == KVT - 1,
                                             release=rel and k == 0 and i == 0)
                        mm.then_inc(proj_full, 1)

                def pair(p, last):
                    others(p)

                    def scores(i):
                        head, q0, (k0, nk) = Q_TILES[i]
                        if i == 0:
                            pe.wait_ge(part_done, p * PROJ + (LAT_PARTS + VAL))
                        pe.wait_ge(s_exp, p * 12 + max(i - 2, 0))
                        out = ps[:, SCORE_BANKS[i % SCORE_BUFS], 0:nk]
                        qs, ks = slice(q0, q0 + P), slice(k0, k0 + nk)
                        mm3(out, both(qn_r, head, qs), both(kn_r, head, ks), True, False, release=(i == 0))
                        r = slice(head * ROPE, (head + 1) * ROPE)
                        mm3(out, [qr_r[r, j, qs] for j in range(2)], [h[r, j, KR, ks] for j in range(2)],
                            False, True).then_inc(s_full, 1)

                    def transposes(i):
                        head, q0, (k0, nk) = Q_TILES[i]
                        pe.wait_ge(p_done, p * 12 + (i + 1))
                        for t in range(nk // P):
                            if i % 2 == 0 and t % 2 == 0:
                                j = max([j for j in range(i // 2) if GROUPS[j + 1] - GROUPS[j] > t // 2], default=-1)
                                if j >= 0:
                                    pe.wait_ge(pt_done, p * GROUPS[-1] + (GROUPS[j] + t // 2 + 1))
                            c = (t % 2) * 256 + (i % 2) * P
                            mm = pe.transpose(ps[:, 6 + t // 2, c:c + P], probs[:, i % SCORE_BUFS, t * P:(t + 1) * P],
                                              ident[:, :])
                        mm.then_inc(tr_full, 1)

                    def values(j):
                        head, q0, (k0, nk) = Q_TILES[2 * j]
                        if j == 0:
                            pe.wait_ge(part_done, p * PROJ + (LAT_PARTS + PROJ))
                        if j >= 2:
                            pe.wait_ge(o_done, p * 6 + (j - 1))
                        for t in range(nk // P):
                            if t % 2 == 0:
                                pe.wait_ge(pt_done, p * GROUPS[-1] + (GROUPS[j] + t // 2 + 1))
                            mm = mm3(ps[:, j % 2, 0:256],
                                     [v_r[:, i, k0 // P + t, head * VDIM:(head + 1) * VDIM] for i in range(2)],
                                     [pt[j % 2][i][:, t, :] for i in range(2)], t == 0, t == nk // P - 1)
                        mm.then_inc(pv_full, 1)

                    for i in range(16):
                        if i < 12:
                            scores(i)
                        if 2 <= i < 14:
                            transposes(i - 2)
                        if i >= 5 and i % 2 == 1:
                            if i == 15 and not last:
                                pe.wait_ge(s_exp, p * 12 + 12)
                                early(p + 1)
                            values((i - 5) // 2)

                pe.wait_ge(part_done, 2 * QT)
                early(0)
                with pe.Fori(0, PAIRS - 1) as p:
                    pair(p, False)
                pair(PAIRS - 1, True)

            pe.wait_ge(mean_ready, 3)
            for b, (kind, unit, q, d) in enumerate(todo):
                up_start(b, unit, q)
                if kind == "ffn":
                    for n, (c0, nc_) in enumerate(BLOCKS):
                        ub, qb, db = unit + 2 * c0 + KT * n, q + 2 * c0, d + 2 * KT * n
                        with pe.Fori(1 if n == 0 else 0, nc_ // 2) as i:
                            up_pair(i * 4 + qb, i * 4 + ub, ub)
                        made = ffn_items(b) + 2 * (c0 + nc_)
                        need = ((h_done, made - 1), (h_done, made))
                        ub += 2 * nc_
                        if n < len(BLOCKS) - 1:
                            with pe.Fori(0, KT // 4) as i:
                                out_items(i * 8 + db, i * 4 + ub, ub, h, nc_, OUTS[:8], need=need)
                        else:
                            out_items(db, ub, ub, h, nc_, LAST_OUTS, need=need, last_of=b)
                elif kind == "conv":
                    conv_taps(0, 0)
                    for half in range(2):
                        pe.matmul(ps[:, SPREAD_BANK + half, 0:HALF], mean_w[:, :],
                                  zero[:, 0:1].broadcast_to([P, HALF]), start=True, stop=False)
                    with pe.Fori(1, KT // 2) as i:
                        for j in range(2):
                            up_pair(i * 4 + q, i * 4 + unit, unit, (2 * j, 2 * j + 1))
                            conv_taps(i * 2 + (j - 1), 1 - j)
                            mean(i * 2 + (j - 2))
                    conv_taps(KT - 1, 1)
                    mean(KT - 2)
                    mean(KT - 1, last=True).then_inc(mean_full, 1)
                    for half in range(2):
                        for k in range(KT):
                            pe.wait_ge(dev_sq, half * KT + k + 1)
                            sums(OUT_BANK + half, 0, DEV_SQ[(half * KT + k) % len(DEV_SQ)], k == 0, k == KT - 1
                                 ).then_inc(dev_sq_used, 1)
                    for half in range(2):
                        spread(norm(b, "inner", half), SPREAD_BANK + half, ln_diag[:, half, :, :])
                    ub = unit + 2 * KT
                    out_items(d, ub, ub, xg, KT, LAST_OUTS, each=ln_split, last_of=b)
                else:
                    attention(b, unit)
                    pe.wait_ge(o_done, 6 * PAIRS)
                    ub = unit + 2 * QT + 4 * PAIRS
                    out_items(d, ub, ub, xg, KT, LAST_OUTS, release_first=False, last_of=b)
            post_square(stages - 1, 1)
            spread(norm(stages - 1, "post", 1))

        @block.scalar
        def _(act):
            def input_hi(b, half, k):
                if b == 0:
                    act.wait_ge(x_loaded[half], 16)
                else:
                    act.wait_ge(x_done, step(b - 1, half, k) + 1)
                act.activation(xg[:, 0, k, cols(half)], x[:, k, cols(half)], ACT.Copy,
                               scale=v(f"pre{b}", k)).then_inc(xg_hi, 1)

            def input_square(b, half, k):
                if half == 1:
                    act.wait_ge(pre_sq_used, step(b, half, k) - 1)
                act.activation(square_place(half, k), x[:, k, cols(half)], ACT.Square).then_inc(pre_sq, 1)

            def output_square(d, n, m, half):
                act.wait_ge(y_done, d + (n + 1 + CREDIT))
                act.activation(sq[:, n % 2, :], y[:, m, cols(half)], ACT.Square).then_inc(sq_done, 1)

            def ffn_item(q, g, par, c, half):
                act.wait_ge(scaled, q + 1)
                act.activation(act_out[:, par, :], gu[:, par, 0, :], ACT.Silu).then_inc(act_done, 1)
                act.wait_ge(prod_done, g + 1)
                act.activation(h[:, 0, at(c), cols(half)], prod[:, par:par + 1, :], ACT.Copy).then_inc(h_hi, 1)

            def conv_item(q, par, c):
                act.wait_ge(scaled, q + 1)
                act.activation(carrier[:, par:1 + par], gu[:, par, 1, 0:1], ACT.Copy)
                act.activation(act_out[:, par, :], gu[:, par, 1, :], ACT.Sigmoid,
                               bias=v("b_pw1", c + KT)).then_inc(act_done, 1)

            def tap_weights(c, slot):
                if not isinstance(c, int) or c >= 2:
                    act.wait_ge(taps_full, c - 1)
                act.activation(carrier[:, 2 + slot:3 + slot], ident[:, 0:1], ACT.Copy)
                for i in range(PE_TAPS):
                    ins = act.activation(tap_w[:, slot, i, :], ident[:, :], ACT.Copy,
                                         scale=v("w_dw", c * TAPS + (DVE_TAPS + i)))
                ins.then_inc(tap_w_ready, 1)

            def start(b, d):
                for k in range(KT - 2):
                    if b > 0 and k in (2, 5):
                        n = 13 if k == 2 else 14
                        output_square(d, n, *LAST_OUTS[n])
                    input_hi(b, 0, k)
                    input_square(b, 0, k)
                for k in (KT - 2, KT - 1):
                    input_hi(b, 0, k)
                if b > 0:
                    output_square(d, 15, *LAST_OUTS[15])
                    act.wait_ge(acc_done, 2 * b)
                for k in (KT - 2, KT - 1):
                    input_square(b, 0, k)
                for k in range(4):
                    input_hi(b, 1, k)
                for k in range(KT):
                    input_square(b, 1, k)
                    if 1 <= k < 5:
                        input_hi(b, 1, k + 3)

            def swap(src, half):
                for g in range(4):
                    to = g ^ 1
                    ins = act.activation(rope_tmp[32 * to:32 * to + 32, 0, :], src[32 * g:32 * g + 32],
                                         ACT.Copy)
                ins.then_inc(swapped, 1)

            def attention(b, q):
                act.wait_ge(x_done, step(b, 0, 0))
                act.dma_start(x_kept, x[:, :, :]).then_inc(x_saved, 16)
                act.wait_ge(pre_sq_used, step(b, 1, KT - 1) + 1)
                for n, (j, half) in enumerate(STARTING + ((2, 0), (2, 1))):
                    act.wait_ge(scaled, q + n + 1)
                    for t in (2 * j, 2 * j + 1):
                        if t < LATENTS:
                            act.activation(LAT_SQ[2 * t + half], y[:, t, cols(half)], ACT.Square
                                           ).then_inc(lat_sq, 1)
                act.dma_start(table[:, :, :], rope_in).then_inc(table_loaded, 16)
                for n in range(2 * LATENTS):
                    act.wait_ge(lat_f, n + 1)
                    act.activation(h[:, 0, n // 2, cols(n % 2)], prod[:, n % 2, :], ACT.Copy).then_inc(part_hi, 1)
                act.wait_ge(part_done, 2 * LATENTS)
                for half in range(2):
                    if half == 1:
                        act.wait_ge(part_done, 2 * LATENTS + 1)
                    swap(y[:, KR, cols(half)], half)
                    act.wait_ge(rotated, half + 1)
                    act.activation(h[:, 0, KR, cols(half)], rope_tmp[:, 3, :], ACT.Copy).then_inc(part_hi, 1)
                act.wait_ge(x_saved, 16)

                def hi_part(p, n):
                    act.wait_ge(proj_full, p * PROJ + (n + 1))
                    bank, half = PROJ_BANKS[n], n % 2
                    if n < QUERY:
                        act.wait_ge(rotated, p * 2 + (n + 3))
                        to, src = qr_r[:, 0, cols(half)], rope_tmp[:, 3, :]
                    elif n < KEY:
                        to, src = qn_r[:, 0, (n - QUERY) // 2, cols(half)], ps[:, bank, 0:HALF]
                    elif n < VAL:
                        to, src = kn_r[:, 0, (n - KEY) // 2, cols(half)], ps[:, bank, 0:HALF]
                    else:
                        t = (n - VAL) * 2
                        to, src = v_r[:, 0, t:t + 2, :], ps[:, bank, :].rearrange("p (a n) -> p a n", a=2)
                    act.activation(to, src, ACT.Copy).then_inc(part_hi, 1)

                def swap_queries(p, half):
                    act.wait_ge(proj_full, p * PROJ + (half + 1))
                    if half == 0:
                        act.wait_ge(part_done, p * PROJ + LAT_PARTS)
                    else:
                        act.wait_ge(rotated, p * 2 + 3)
                    swap(ps[:, PROJ_BANKS[half], 0:HALF], half)

                def early(p):
                    for n in PARTS[:EARLY]:
                        if n < QUERY:
                            swap_queries(p, n)
                        hi_part(p, n)

                def pair(p, last):
                    for n in PARTS[EARLY:]:
                        hi_part(p, n)

                    def expo(i):
                        nk = Q_TILES[i][2][1]
                        act.wait_ge(s_nmax, p * 12 + (i + 1))
                        act.wait_ge(tr_full, p * 12 + max(i - 2, 0))
                        s = i % SCORE_BUFS
                        act.activation(probs[:, s, 0:nk], ps[:, SCORE_BANKS[s], 0:nk], ACT.Exp,
                                       bias=soft[:, 1, s:s + 1], scale=SCALE,
                                       accum_out=soft[:, 2, s:s + 1]).then_inc(s_exp, 1)

                    def turned(j):
                        nk = Q_TILES[2 * j][2][1]
                        act.wait_ge(tr_full, p * 12 + (2 * j + 2))
                        act.wait_ge(pv_full, p * 6 + max(j - 1, 0))
                        for g in range(nk // 256):
                            act.activation(pt[j % 2][0][:, 2 * g:2 * g + 2, :],
                                           ps[:, 6 + g, :].rearrange("p (a n) -> p a n", a=2), ACT.Copy
                                           ).then_inc(pt_hi, 1)

                    def output(j):
                        head, q0, _ = Q_TILES[2 * j]
                        act.wait_ge(pv_full, p * 6 + (j + 1))
                        act.activation(xg[:, 0, at(p * 2 + head), q0:q0 + 256], ps[:, j % 2:j % 2 + 1, 0:256],
                                       ACT.Copy).then_inc(o_hi, 1)

                    for i in range(17):
                        if i < 12:
                            expo(i)
                        if i >= 3 and i % 2 == 1 and i < 15:
                            turned((i - 3) // 2)
                        if i >= 6 and i % 2 == 0:
                            if i == 16 and not last:
                                early(p + 1)
                            output((i - 6) // 2)

                early(0)
                with act.Fori(0, PAIRS - 1) as p:
                    pair(p, False)
                pair(PAIRS - 1, True)
                act.wait_ge(o_done, 6 * PAIRS)
                act.dma_start(x[:, :, :], x_kept).then_inc(x_back, 16)

            act.dma_start(x[:, :, cols(0)], x_in[:, :, cols(0)]).then_inc(x_loaded[0], 16)
            act.wait_ge(vec_loaded, 16)
            start(0, 0)
            for b, (kind, unit, q, d) in enumerate(todo):
                g = ffn_items(b)
                if kind == "ffn":
                    for n, (c0, nc_) in enumerate(BLOCKS):
                        qb, gb = q + 2 * c0, g + 2 * c0
                        if n == 0:
                            for m, (j, half) in enumerate(STARTING):
                                ffn_item(qb + m, gb + m, m % 2, j, half)
                        with act.Fori(1 if n == 0 else 0, nc_ // 2) as i:
                            for m, (j, half) in enumerate(STEADY):
                                ffn_item(i * 4 + (qb + m), i * 4 + (gb + m), m % 2, i * 2 + j, half)
                    d += 2 * KT * (len(BLOCKS) - 1)
                elif kind == "conv":
                    for c in range(2):
                        tap_weights(c, c)
                    for m, (j, half) in enumerate(STARTING):
                        conv_item(q + m, m % 2, j)
                    with act.Fori(1, KT // 2) as i:
                        for m, (j, half) in enumerate(STEADY):
                            conv_item(i * 4 + (q + m), m % 2, i * 2 + j)
                            if half == 1:
                                tap_weights(i * 2 + j, j)
                    for n in range(2 * KT):
                        half, k = n // KT, n % KT
                        act.wait_ge(centred, n + 1)
                        if n >= len(DEV_SQ):
                            act.wait_ge(dev_sq_used, n + 1 - len(DEV_SQ))
                        act.activation(DEV_SQ[n % len(DEV_SQ)], y[:, k, cols(half)], ACT.Square).then_inc(dev_sq, 1)
                    for n in range(2 * KT):
                        half, k = n // KT, n % KT
                        act.wait_ge(ln_done, n + 1)
                        if n >= 2:
                            act.wait_ge(ln_split, n - 1)
                        act.activation(act_out[:, k % 2, :], prod[:, k % 2, :], ACT.Silu,
                                       bias=v("ln_b", k)).then_inc(ln_act, 1)
                        act.wait_ge(ln_act, n + 1)
                        act.activation(xg[:, 0, k, cols(half)], act_out[:, k % 2, :], ACT.Copy).then_inc(ln_hi, 1)
                else:
                    attention(b, q)
                for n, (m, half) in enumerate(LAST_OUTS):
                    if n < 13 or b + 1 == stages:
                        output_square(d, n, m, half)
                if b + 1 < stages:
                    start(b + 1, d)

        @block.vector
        def _(dve):
            steps = [0]

            def stepped(ins):
                steps[0] += 1
                ins.then_inc(newton_step, 1)

            def read_sums(src, c0, n, count):
                dve.tensor_scalar(newton[:, 0, c0:c0 + n], src, 1.0 / count, EPS, ALU.mult, ALU.add
                                  ).then_inc(sums_read, 1)

            def root_step(i, n):
                v_, r, a, b_ = (newton[:, j, 0:n] for j in range(4))
                if i > 0:
                    dve.wait_ge(newton_step, steps[0])
                if i == 0:
                    stepped(dve.tensor_scalar(a.bitcast(I32), v_.bitcast(I32), 1, None, ALU.logical_shift_right))
                elif i == 1:
                    stepped(dve.tensor_scalar(r.bitcast(I32), a.bitcast(I32), -1.0, float(0x5F3759DF),
                                              ALU.mult, ALU.add))
                elif i % 3 == 2:
                    stepped(dve.scalar_tensor_tensor(a, r, -0.5, r, ALU.mult, ALU.mult))
                elif i % 3 == 0:
                    stepped(dve.tensor_tensor(b_, a, v_, ALU.mult))
                else:
                    stepped(dve.scalar_tensor_tensor(r, b_, 1.5, r, ALU.add, ALU.mult))

            def inverse_root(n):
                for i in range(ROOT_STEPS):
                    root_step(i, n)
                dve.wait_ge(newton_step, steps[0])

            def diagonals(to, c0):
                for c in range(TT):
                    ins = dve.tensor_scalar(to[:, c, :], ident[:, :], newton[:, 1, c0 + c:c0 + c + 1], None, ALU.mult)
                ins.then_inc(diag_ready, 1)

            copied = [0]

            def take_spread(no, out):
                dve.wait_ge(spread_full, no + 1)
                dve.tensor_copy(out, ps[:, SPREAD_BANK, 0:HALF]).then_inc(rms_done, 1)
                copied[0] += 1
                dve.wait_ge(rms_done, copied[0])

            def pre_read(b, half):
                dve.wait_ge(pre_sums_full, 2 * b + half + 1)
                read_sums(ps[:, SUM_BANK, 0:TT], 0, TT, D_MODEL)
                dve.wait_ge(sums_read, norm(b, "pre", half) + 1)

            def pre_rms(b, half):
                inverse_root(TT)
                diagonals(diag, 0)
                take_spread(norm(b, "pre", half), r_pre[:, half, :])

            def post_root(b, half):
                no = norm(b, "post", half)
                dve.wait_ge(sums_full, 2 * b + 4 * (b > 3) + half + 1)
                read_sums(ps[:, SPREAD_BANK, 0:TT], 0, TT, D_MODEL)
                dve.wait_ge(sums_read, no + 1)
                inverse_root(TT)
                diagonals(diag, 0)

            def input_lo(b, half, k):
                dve.wait_ge(xg_hi, step(b, half, k) + 1)
                dve.scalar_tensor_tensor(xg[:, 1, k, cols(half)], x[:, k, cols(half)], v(f"pre{b}", k),
                                         xg[:, 0, k, cols(half)].bitcast(F32), ALU.mult, ALU.subtract
                                         ).then_inc(xg_done, 1)

            def apply(b, half, ks, root=False):
                if SUBLAYERS[b][0] == "ffn":
                    gamma, c = half_post, KT * b
                else:
                    gamma, c = vec, VEC["post0"] + KT * b
                pre = b + 1 < stages
                n = len(ks)
                for j in range(n + 2):
                    if j < n:
                        k = ks[j]
                        if step(b, half, k) >= 2:
                            dve.wait_ge(x_done, step(b, half, k) - 1)
                        dve.scalar_tensor_tensor(prod[:, k % 2, :], y[:, k, cols(half)],
                                                 gamma[:, c + k:c + k + 1], r_post[:, half, :],
                                                 ALU.mult, ALU.mult).then_inc(t_ready, 1)
                    if 1 <= j <= n:
                        k = ks[j - 1]
                        dve.wait_ge(t_ready, step(b, half, k) + 1)
                        dve.tensor_tensor(x[:, k, cols(half)], x[:, k, cols(half)], prod[:, k % 2, :],
                                          ALU.add).then_inc(x_done, 1)
                    if root and j == 1:
                        pre_read(b + 1, 0)
                    if root and 2 <= j < 8:
                        root_step(2 * j - 4, TT)
                    if pre and j >= 2:
                        input_lo(b + 1, half, ks[j - 2])
                    if root and 2 <= j and 2 * j - 3 < ROOT_STEPS:
                        root_step(2 * j - 3, TT)

            def scale_item(kind, q, bank, par, j, half):
                dve.wait_ge(up_full, q + 1)
                dst = y[:, 2 * j:2 * j + 2, cols(half)] if kind == "mla" else gu[:, par, :, :]
                dve.tensor_tensor(dst, ps[:, bank:bank + 2, 0:HALF],
                                  r_pre[:, half:half + 1, :].broadcast_to([P, 2, HALF]), ALU.mult
                                  ).then_inc(scaled, 1)

            def ffn_item(a, g, par, c, half):
                dve.wait_ge(act_done, a + 1)
                dve.tensor_tensor(prod[:, par, :], act_out[:, par, :], gu[:, par, 1, :], ALU.mult
                                  ).then_inc(prod_done, 1)
                dve.wait_ge(h_hi, g + 1)
                dve.tensor_tensor(h[:, 1, at(c), cols(half)], prod[:, par:par + 1, :],
                                  h[:, 0, at(c), cols(half)].bitcast(F32), ALU.subtract).then_inc(h_done, 1)

            def take_out(d, n, m, half, first, bias=None):
                dve.wait_ge(out_full, d + (n + 1))
                dst = y[:, at(m), cols(half)]
                src = ps[:, OUT_BANK + n % 2:OUT_BANK + n % 2 + 1, 0:HALF]
                if bias is not None:
                    dve.tensor_scalar(dst, src, bias, None, ALU.add).then_inc(y_done, 1)
                elif first:
                    dve.tensor_copy(dst, src).then_inc(y_done, 1)
                else:
                    dve.tensor_tensor(dst, dst, src, ALU.add).then_inc(y_done, 1)

            def sum_square(b, n, m, half):
                dve.wait_ge(sq_done, 2 * KT * b + n + 1)
                if m == 0:
                    ins = dve.tensor_copy(acc[:, half, :], sq[:, n % 2, :])
                else:
                    ins = dve.tensor_tensor(acc[:, half, :], acc[:, half, :], sq[:, n % 2, :], ALU.add)
                if m == KT - 1:
                    ins.then_inc(acc_done, 1)

            def finish(b, d, first, bias):
                for n, (m, half) in enumerate(LAST_OUTS):
                    if n == 12:
                        post_root(b, 0)
                    if n == 13:
                        take_spread(norm(b, "post", 0), r_post[:, 0, :])
                        if SUBLAYERS[b][0] == "mla":
                            dve.wait_ge(x_back, 16)
                        apply(b, 0, range(2))
                    if n == 14:
                        apply(b, 0, range(2, 5))
                    take_out(d, n, m, half, first, v(bias, m) if bias else None)
                    if n == 14:
                        apply(b, 0, range(5, KT))
                    sum_square(b, n, m, half)
                post_root(b, 1)
                take_spread(norm(b, "post", 1), r_post[:, 1, :])
                apply(b, 1, range(KT), root=b + 1 < stages)
                if b + 1 < stages:
                    dve.wait_ge(newton_step, steps[0])
                    diagonals(diag, 0)
                    take_spread(norm(b + 1, "pre", 0), r_pre[:, 0, :])
                    kind, _, q, _ = SUBLAYERS[b + 1]
                    scale_item(kind, q, START_BANKS[0], 0, 0, 0)
                    scale_item(kind, q + 1, START_BANKS[1], 1, 1, 0)

            def glu(a, par, c, half, slot):
                dve.wait_ge(act_done, a + 1)
                spans = (((0, PROMPT, PAD), (PROMPT, HALF, SEG + PAD)) if half == 0
                         else ((0, HALF, SEG + PAD + HALF - PROMPT),))
                for f, t, to in spans:
                    dve.scalar_tensor_tensor(cin[:, slot, to:to + t - f], gu[:, par, 0, f:t], v("b_pw1", c),
                                             act_out[:, par, f:t], ALU.add, ALU.mult).then_inc(conv_in, 1)

            def depthwise(c, slot):
                if not isinstance(c, int) or c > 0:
                    dve.wait_ge(conv_done, c)
                for j in range(DVE_TAPS):
                    src, out = cin[:, slot, j:j + CONV_OUT], cacc[:, j % 2, :]
                    w = v("w_dw", c * TAPS + j)
                    if j >= 2:
                        dve.wait_ge(tap_done, c * DVE_TAPS + (j - 1))
                        ins = dve.scalar_tensor_tensor(out, src, w, out, ALU.mult, ALU.add)
                    elif j == 1:
                        ins = dve.tensor_scalar(out, src, w, None, ALU.mult)
                    else:
                        ins = dve.tensor_scalar(out, src, w, v("b_dw", c), ALU.mult, ALU.add)
                    ins.then_inc(tap_done, 1)
                dve.wait_ge(tap_done, c * DVE_TAPS + DVE_TAPS)
                dve.tensor_tensor(cacc[:, 0, :], cacc[:, 0, :], cacc[:, 1, :], ALU.add).then_inc(chains_done, 1)

            def convolved(c):
                dve.wait_ge(chains_done, c + 1)
                dve.wait_ge(taps_full, c + 1)
                dve.tensor_tensor(y[:, at(c), 0:PROMPT], cacc[:, 0:1, 0:PROMPT],
                                  ps[:, OUT_BANK:OUT_BANK + 1, 0:PROMPT], ALU.add)
                dve.tensor_tensor(y[:, at(c), PROMPT:TOK], cacc[:, 0:1, SEG:CONV_OUT],
                                  ps[:, OUT_BANK + 1:OUT_BANK + 2, 0:SAMPLE], ALU.add).then_inc(conv_done, 1)

            def layer_norm():
                dve.wait_ge(mean_full, 1)
                for n in range(2 * KT):
                    half, k = n // KT, n % KT
                    dve.tensor_tensor(y[:, k, cols(half)], y[:, k, cols(half)], ps[:, SPREAD_BANK + half, 0:HALF],
                                      ALU.subtract).then_inc(centred, 1)

                dve.wait_ge(dev_sq_used, 2 * KT)
                for half in range(2):
                    read_sums(ps[:, OUT_BANK + half, 0:TT], half * TT, TT, D_MODEL)
                dve.wait_ge(sums_read, norm(1, "inner", 1) + 1)
                inverse_root(2 * TT)
                for half in range(2):
                    diagonals(ln_diag[:, half, :, :], half * TT)

                def ln_lo(n):
                    half, k = n // KT, n % KT
                    dve.wait_ge(ln_hi, n + 1)
                    dve.tensor_tensor(xg[:, 1, k, cols(half)], act_out[:, k % 2, :],
                                      xg[:, 0, k, cols(half)].bitcast(F32), ALU.subtract).then_inc(ln_split, 1)

                for n in range(2 * KT):
                    half, k = n // KT, n % KT
                    if k == 0:
                        dve.wait_ge(spread_full, norm(1, "inner", half) + 1)
                    if n >= 2:
                        dve.wait_ge(ln_act, n - 1)
                    dve.scalar_tensor_tensor(prod[:, k % 2, :], y[:, k, cols(half)], v("ln_g", k),
                                             ps[:, SPREAD_BANK + half, 0:HALF], ALU.mult, ALU.mult).then_inc(ln_done, 1)
                    if n >= 1:
                        ln_lo(n - 1)
                ln_lo(2 * KT - 1)

            def rotate(src, half, n):
                dve.wait_ge(swapped, n + 1)
                dve.tensor_tensor(rope_tmp[:, 1, :], src, table[:, 0, cols(half)], ALU.mult).then_inc(rope_part, 1)
                dve.tensor_tensor(rope_tmp[:, 2, :], rope_tmp[:, 0, :], table[:, 1, cols(half)], ALU.mult
                                  ).then_inc(rope_part, 1)
                dve.wait_ge(rope_part, n * 2 + 2)
                dve.tensor_tensor(rope_tmp[:, 3, :], rope_tmp[:, 1, :], rope_tmp[:, 2, :], ALU.add
                                  ).then_inc(rotated, 1)

            def attention(b, q):
                for n in range(4, 6):
                    scale_item("mla", q + n, STEADY_BANKS[n - 4], 0, 2, n - 4)
                dve.wait_ge(sums_full, 2 * b + 4)
                read_sums(ps[:, SUM_BANK, 0:2 * TT], 0, 2 * TT, Q_RANK)
                read_sums(ps[:, SUM_BANK, 2 * TT:4 * TT], 2 * TT, 2 * TT, KV_RANK)
                for g in range(2):
                    dve.tensor_copy(newton[:, 3, g:g + 1], ident[:, 0:1]).then_inc(sums_read, 1)
                dve.wait_ge(sums_read, norm(b, "inner") + 4)
                inverse_root(4 * TT)
                for g in range(4):
                    diagonals(lat_diag[:, g, :, :], g * TT)
                dve.wait_ge(spread_full, norm(b, "inner") + 4)

                def lat_lo(n):
                    dve.wait_ge(part_hi, n + 1)
                    dve.tensor_tensor(h[:, 1, n // 2, cols(n % 2)], prod[:, n % 2, :],
                                      h[:, 0, n // 2, cols(n % 2)].bitcast(F32), ALU.subtract
                                      ).then_inc(part_done, 1)

                for n in range(2 * LATENTS):
                    t, half = n // 2, n % 2
                    gamma = v("q_g", t) if t < QT else v("kv_g", t - QT)
                    if n >= 2:
                        dve.wait_ge(part_done, n - 1)
                    dve.scalar_tensor_tensor(prod[:, half, :], y[:, t, cols(half)], gamma,
                                             ps[:, LAT_BANKS[2 * (t >= QT) + half], 0:HALF], ALU.mult, ALU.mult
                                             ).then_inc(lat_f, 1)
                    if n >= 1:
                        lat_lo(n - 1)
                lat_lo(2 * LATENTS - 1)
                dve.wait_ge(table_loaded, 16)
                for half in range(2):
                    rotate(y[:, KR, cols(half)], half, half)
                    dve.wait_ge(part_hi, 2 * LATENTS + half + 1)
                    dve.tensor_tensor(h[:, 1, KR, cols(half)], rope_tmp[:, 3, :],
                                      h[:, 0, KR, cols(half)].bitcast(F32), ALU.subtract).then_inc(part_done, 1)
                dve.wait_ge(x_saved, 16)

                def lo_part(p, n):
                    bank, half = PROJ_BANKS[n], n % 2
                    dve.wait_ge(part_hi, p * PROJ + (LAT_PARTS + PARTS.index(n) + 1))
                    src = ps[:, bank, 0:HALF]
                    if n < QUERY:
                        hi, lo = (qr_r[:, i, cols(half)] for i in range(2))
                        src = rope_tmp[:, 3, :]
                    elif n < KEY:
                        hi, lo = (qn_r[:, i, (n - QUERY) // 2, cols(half)] for i in range(2))
                    elif n < VAL:
                        hi, lo = (kn_r[:, i, (n - KEY) // 2, cols(half)] for i in range(2))
                    else:
                        t = (n - VAL) * 2
                        hi, lo = (v_r[:, i, t:t + 2, :] for i in range(2))
                        src = ps[:, bank, :].rearrange("p (a n) -> p a n", a=2)
                    dve.tensor_tensor(lo, src, hi.bitcast(F32), ALU.subtract).then_inc(part_done, 1)

                def rotate_queries(p, half):
                    dve.wait_ge(proj_full, p * PROJ + (half + 1))
                    rotate(ps[:, PROJ_BANKS[half], 0:HALF], half, p * 2 + (half + 2))

                def early(p):
                    for n in PARTS[:EARLY]:
                        if n < QUERY:
                            rotate_queries(p, n)
                        lo_part(p, n)

                def pair(p, last):
                    for n in PARTS[EARLY:]:
                        lo_part(p, n)

                    def row_max(i):
                        nk, s = Q_TILES[i][2][1], i % SCORE_BUFS
                        dve.wait_ge(s_full, p * 12 + (i + 1))
                        dve.tensor_reduce(soft[:, 0, s:s + 1], ps[:, SCORE_BANKS[s], 0:nk], AX_X, ALU.max).then_inc(s_max, 1)
                        dve.wait_ge(s_max, p * 12 + (i + 1))
                        dve.tensor_scalar(soft[:, 1, s:s + 1], soft[:, 0, s:s + 1], -SCALE, None, ALU.mult
                                          ).then_inc(s_nmax, 1)

                    def divide(i):
                        nk, s = Q_TILES[i][2][1], i % SCORE_BUFS
                        dve.wait_ge(s_exp, p * 12 + (i + 1))
                        dve.reciprocal(soft[:, 3, s:s + 1], soft[:, 2, s:s + 1]).then_inc(s_inv, 1)
                        dve.wait_ge(s_inv, p * 12 + (i + 1))
                        dve.tensor_scalar(probs[:, s, 0:nk], probs[:, s, 0:nk], soft[:, 3, s:s + 1], None,
                                          ALU.mult).then_inc(p_done, 1)

                    def turned(j):
                        nk = Q_TILES[2 * j][2][1]
                        for g in range(nk // 256):
                            dve.wait_ge(pt_hi, p * GROUPS[-1] + (GROUPS[j] + g + 1))
                            dve.tensor_tensor(pt[j % 2][1][:, 2 * g:2 * g + 2, :],
                                              ps[:, 6 + g, :].rearrange("p (a n) -> p a n", a=2),
                                              pt[j % 2][0][:, 2 * g:2 * g + 2, :].bitcast(F32),
                                              ALU.subtract).then_inc(pt_done, 1)

                    def output(j):
                        head, q0, _ = Q_TILES[2 * j]
                        dve.wait_ge(o_hi, p * 6 + (j + 1))
                        dve.tensor_tensor(xg[:, 1, at(p * 2 + head), q0:q0 + 256], ps[:, j % 2:j % 2 + 1, 0:256],
                                          xg[:, 0, at(p * 2 + head), q0:q0 + 256].bitcast(F32), ALU.subtract
                                          ).then_inc(o_done, 1)

                    for i in range(18):
                        if i >= 4 and i % 2 == 0 and i < 16:
                            turned((i - 4) // 2)
                        if i < 12:
                            row_max(i)
                        if 1 <= i < 13:
                            divide(i - 1)
                        if i >= 7 and i % 2 == 1:
                            if i == 17 and not last:
                                early(p + 1)
                            output((i - 7) // 2)

                early(0)
                with dve.Fori(0, PAIRS - 1) as p:
                    pair(p, False)
                pair(PAIRS - 1, True)

            dve.wait_ge(vec_loaded, 16)
            dve.tensor_scalar(half_post[:, :], vec[:, VEC["post0"]:VEC["post0"] + 6 * KT], 0.5, None,
                              ALU.mult).then_inc(consts, 1)
            for i in range(CREDIT):
                dve.memset(acc[:, i, :], 0.0).then_inc(y_done, 1)
            for k in range(KT):
                input_lo(0, 0, k)
            pre_read(0, 0)
            dve.wait_ge(ident_loaded, 16)
            for k in range(KT):
                input_lo(0, 1, k)
            pre_rms(0, 0)
            scale_item("ffn", 0, START_BANKS[0], 0, 0, 0)
            scale_item("ffn", 1, START_BANKS[1], 1, 1, 0)
            dve.wait_ge(consts, 1)
            for b, (kind, unit, q, d) in enumerate(todo):
                g, a = ffn_items(b), act_items(b)
                if kind == "ffn":
                    for n, (c0, nc_) in enumerate(BLOCKS):
                        qb, gb, ab, db = q + 2 * c0, g + 2 * c0, a + 2 * c0, d + 2 * KT * n
                        if n == 0:
                            for m, (j, half) in enumerate(STARTING):
                                if m == 2:
                                    pre_read(b, 1)
                                    pre_rms(b, 1)
                                if m >= 2:
                                    scale_item(kind, qb + m, START_BANKS[m], m % 2, j, half)
                                ffn_item(ab + m, gb + m, m % 2, j, half)
                        with dve.Fori(1 if n == 0 else 0, nc_ // 2) as i:
                            for m, (j, half) in enumerate(STEADY):
                                scale_item(kind, i * 4 + (qb + m), STEADY_BANKS[m], m % 2, j, half)
                                ffn_item(i * 4 + (ab + m), i * 4 + (gb + m), m % 2, i * 2 + j, half)
                        if n < len(BLOCKS) - 1:
                            with dve.Fori(0, KT // 4) as i:
                                for m in range(8):
                                    take_out(i * 8 + db, m, i * 4 + m // 2, m % 2, n == 0)
                    finish(b, d + 2 * KT * (len(BLOCKS) - 1), False, None)
                elif kind == "conv":
                    dve.memset(cin[:, :, :], 0.0).then_inc(pads, 1)
                    dve.wait_ge(pads, 1)
                    for m, (j, half) in enumerate(STARTING):
                        if m == 2:
                            pre_read(b, 1)
                            pre_rms(b, 1)
                        if m >= 2:
                            scale_item(kind, q + m, START_BANKS[m], m % 2, j, half)
                        glu(a + m, m % 2, j, half, j)
                    dve.wait_ge(conv_in, 6)
                    depthwise(0, 0)
                    convolved(0)
                    depthwise(1, 1)
                    with dve.Fori(1, KT // 2) as i:
                        for m, (j, half) in enumerate(STEADY):
                            scale_item(kind, i * 4 + (q + m), STEADY_BANKS[m], m % 2, j, half)
                            glu(i * 4 + (a + m), m % 2, i * 2 + j, half, j)
                            if half == 1:
                                convolved(i * 2 + (j - 1))
                                dve.wait_ge(conv_in, i * 6 + (3 * j + 3))
                                depthwise(i * 2 + j, j)
                    convolved(KT - 1)
                    layer_norm()
                    finish(b, d, False, "b_pw2")
                else:
                    for m in range(2, 4):
                        if m == 2:
                            pre_read(b, 1)
                            pre_rms(b, 1)
                        scale_item(kind, q + m, START_BANKS[m], 0, STARTING[m][0], 1)
                    attention(b, q)
                    finish(b, d, True, None)


WEIGHT_SETS = (("ffn", "l0_ffn1_"), ("conv", "l0_conv_"), ("ffn", "l0_ffn2_"),
               ("ffn", "l1_ffn1_"), ("mla", "l1_mla_"), ("ffn", "l1_ffn2_"))
PRE = ("l0_ffn1_pre_g", "l0_mix_pre_g", "l0_ffn2_pre_g", "l1_ffn1_pre_g", "l1_mix_pre_g", "l1_ffn2_pre_g")
POST = tuple(n.replace("_pre_", "_post_") for n in PRE)


def kernel(**inputs):
    import numpy as np
    import concourse.bacc as bacc
    from concourse.bass_utils import run_bass_kernel_spmd

    a = {k: np.asarray(t) for k, t in inputs.items()}

    def tiles(w, m):
        return w[:, m * P:(m + 1) * P].reshape(-1, P, P).transpose(1, 0, 2)

    units = np.zeros((UNITS, P, KT, P), np.float32)
    u = 0

    def put(t):
        nonlocal u
        units[u, :, :t.shape[1]] = t
        u += 1

    for kind, pre in WEIGHT_SETS:
        if kind == "ffn":
            gate, up, down = (a[pre + n] for n in ("w_gate", "w_up", "w_down"))
            for c0, nc_ in BLOCKS:
                for c in range(c0, c0 + nc_):
                    put(tiles(gate, c))
                    put(tiles(up, c))
                for m in range(KT):
                    put(tiles(down, m)[:, c0:c0 + nc_])
        elif kind == "conv":
            for c in range(KT):
                put(tiles(a[pre + "w_pw1"], c))
                put(tiles(a[pre + "w_pw1"], KT + c))
            for m in range(KT):
                put(tiles(a[pre + "w_pw2"], m))
        else:
            dq, dkv, uq = a[pre + "w_dq"], a[pre + "w_dkv"], a[pre + "w_uq"]
            for m in range(QT):
                put(tiles(dq, m))
            for m in range(KVT):
                put(tiles(dkv, m))
            key = dkv[:, KV_RANK:]
            put(tiles(np.concatenate([key, key], 1), 0))
            uq = uq.reshape(Q_RANK, HEADS, NOPE + ROPE)
            for p in range(PAIRS):
                heads = (2 * p, 2 * p + 1)
                put(tiles(np.concatenate([uq[:, i, NOPE:] for i in heads], 1), 0))
                put(np.concatenate([tiles(uq[:, i, :NOPE], 0) for i in heads], 1))
                put(np.concatenate([tiles(a[pre + "w_uk"], i) for i in heads], 1))
                uv = a[pre + "w_uv"][:, heads[0] * VDIM:(heads[1] + 1) * VDIM]
                put(uv.reshape(KVT, P, 2, P).transpose(1, 0, 2, 3).reshape(P, 2 * KVT, P))
            for m in range(KT):
                put(tiles(a[pre + "w_o"], m))
    assert u == UNITS

    vectors = np.zeros((P, VECS), np.float32)

    def column(name, t):
        t = t.reshape(-1, P).T
        vectors[:, VEC[name]:VEC[name] + t.shape[1]] = t

    for i in range(6):
        column(f"pre{i}", a[PRE[i]])
        column(f"post{i}", a[POST[i]])
    for name in ("b_pw1", "b_dw", "ln_g", "ln_b", "b_pw2"):
        column(name, a["l0_conv_" + name])
    column("w_dw", a["l0_conv_w_dw"].reshape(TAPS, KT, P).transpose(1, 0, 2))
    column("q_g", a["l1_mla_q_norm_g"])
    column("kv_g", a["l1_mla_kv_norm_g"])

    freq = (10000.0 ** (-np.arange(0, ROPE, 2) / ROPE)).astype(np.float32)
    place = np.concatenate([np.arange(PROMPT), np.arange(SAMPLE)]).astype(np.float32)
    angle = freq[:, None] * place[None, :]
    cos, sin = np.cos(angle), np.sin(angle)
    rope = np.stack([np.concatenate([cos, cos] * 2), np.concatenate([-sin, sin] * 2)], 1)

    x = np.concatenate([a["x_prompt"][0], a["x_sample"][0]])
    arrays = {"x_in": np.ascontiguousarray(x.T.reshape(KT, P, TOK).transpose(1, 0, 2)),
              "weights": units.reshape(UNITS, P, UNIT), "vectors": vectors,
              "rope_in": np.ascontiguousarray(rope.astype(np.float32)), "ident_in": np.eye(P, dtype=np.float32)}

    nc = bacc.Bacc("TRN2", target_bir_lowering=False, num_devices=1, dynamic_dma_scratch_size=1024)
    args = [nc.dram_tensor(n, t.shape, F32, kind="ExternalInput").ap() for n, t in arrays.items()]
    out = nc.dram_tensor("y_out", (P, KT, TOK), F32, kind="ExternalOutput").ap()
    trunk(nc, *args, out)
    got = run_bass_kernel_spmd(nc, [arrays], core_ids=[0]).results[0]["y_out"]
    y = np.asarray(got).transpose(1, 0, 2).reshape(D_MODEL, TOK).T
    return np.ascontiguousarray(y[:PROMPT])[None], np.ascontiguousarray(y[PROMPT:])[None]
```
